# Optimizing a Trainium2 kernel written in Bass

```python
import math
import jax, jax.numpy as jnp
from jax import lax
import numpy as np
import jax
import jax.numpy as jnp

D_MODEL = 1024
BATCH = 1
SEQ = 256
DEPTH = 1

CHUNK = 64
LEFT_CHUNKS = 8
A_HEADS = 8
A_HEAD_DIM = 64
A_WIDTH = A_HEADS * A_HEAD_DIM
REL_CLIP = 128
B_HEADS = 4
B_HEAD_DIM = 128
B_WIDTH = B_HEADS * B_HEAD_DIM
CONV_K = 4
PEER_HEADS = 8
N_KEYS = 128
N_EXPERTS = N_KEYS * N_KEYS
PEER_TOPK = 16
D_KEY = 256
PEER_BLOCK = 128
EPS = 1e-6
IN_SIZES = [A_WIDTH, A_WIDTH, A_WIDTH, 2 * B_WIDTH, B_WIDTH, B_WIDTH, B_HEADS, B_HEADS, D_MODEL, D_MODEL]
IN_COLS = sum(IN_SIZES)


def rmsnorm(x, g):
    xf = x.astype(jnp.float32)
    y = xf * lax.rsqrt(jnp.mean(xf * xf, axis=-1, keepdims=True) + EPS)
    return (y * g.astype(jnp.float32)).astype(x.dtype)

def modulate(h, shift, scale):
    return h * (1.0 + scale[:, None, :]) + shift[:, None, :]

def causal_depthwise_conv(u, w, b):
    C = u.shape[-1]
    out = lax.conv_general_dilated(
        u, w[:, None, :].astype(u.dtype), window_strides=(1,), padding=[(CONV_K - 1, 0)],
        dimension_numbers=("NWC", "WIO", "NWC"), feature_group_count=C)
    return out + b

def chunk_band_attention(q, k, v, rel_bias):
    B, S, H, dh = q.shape
    nc = S // CHUNK
    pad = LEFT_CHUNKS * CHUNK
    band = pad + CHUNK
    kp = jnp.pad(k, ((0, 0), (pad, 0), (0, 0), (0, 0)))
    vp = jnp.pad(v, ((0, 0), (pad, 0), (0, 0), (0, 0)))
    qc = q.reshape(B, nc, CHUNK, H, dh).transpose(1, 0, 2, 3, 4)
    k_idx = jnp.arange(band)
    rel = jnp.clip(jnp.arange(CHUNK)[:, None] + pad - k_idx[None, :], -REL_CLIP, REL_CLIP) + REL_CLIP
    bias = rel_bias[:, rel].astype(jnp.float32)
    scale = dh ** -0.5

    def one_chunk(args):
        j, qj = args
        kj = lax.dynamic_slice_in_dim(kp, j * CHUNK, band, axis=1)
        vj = lax.dynamic_slice_in_dim(vp, j * CHUNK, band, axis=1)
        s = jnp.einsum("blhd,bkhd->bhlk", qj, kj).astype(jnp.float32) * scale + bias
        valid = (j * CHUNK + k_idx - pad) >= 0
        s = jnp.where(valid[None, None, None, :], s, -jnp.inf)
        p = jax.nn.softmax(s, axis=-1).astype(vj.dtype)
        return jnp.einsum("bhlk,bkhd->blhd", p, vj)

    out = lax.map(one_chunk, (jnp.arange(nc), qc))
    return out.transpose(1, 0, 2, 3, 4).reshape(B, S, H * dh)

def mlstm_chunkwise(q, k, v, i_pre, f_pre):
    B, S, H, d = q.shape
    nc = S // CHUNK
    k = k * (d ** -0.5)
    to_c = lambda t: t.reshape(B, nc, CHUNK, H, d).transpose(1, 0, 3, 2, 4)
    qc, kc, vc = to_c(q), to_c(k), to_c(v)
    li = i_pre.astype(jnp.float32).reshape(B, nc, CHUNK, H).transpose(1, 0, 3, 2)
    lf = jax.nn.log_sigmoid(f_pre.astype(jnp.float32)).reshape(B, nc, CHUNK, H).transpose(1, 0, 3, 2)
    a = jnp.cumsum(lf, axis=-1)
    A = a[..., -1]
    causal = jnp.tril(jnp.ones((CHUNK, CHUNK), dtype=bool))

    def step(carry, inp):
        C, n, m = carry
        qj, kj, vj, aj, Aj, lij = inp
        D = aj[..., :, None] - aj[..., None, :] + lij[..., None, :]
        D = jnp.where(causal, D, -jnp.inf)
        inter = aj + m[..., None]
        m_row = jnp.maximum(inter, jnp.max(D, axis=-1))
        w_inter = jnp.exp(inter - m_row)
        Wd = jnp.exp(D - m_row[..., None])
        qk = jnp.einsum("bhld,bhsd->bhls", qj, kj).astype(jnp.float32) * Wd
        num = w_inter[..., None] * jnp.einsum("bhld,bhde->bhle", qj, C) + jnp.einsum("bhls,bhse->bhle", qk, vj)
        den = w_inter * jnp.einsum("bhld,bhd->bhl", qj, n) + jnp.sum(qk, axis=-1)
        h = num / jnp.maximum(jnp.abs(den), jnp.exp(-m_row))[..., None]
        g = Aj[..., None] - aj + lij
        m_new = jnp.maximum(Aj + m, jnp.max(g, axis=-1))
        decay = jnp.exp(Aj + m - m_new)
        wk = jnp.exp(g - m_new[..., None])
        C_new = decay[..., None, None] * C + jnp.einsum("bhl,bhld,bhle->bhde", wk, kj, vj)
        n_new = decay[..., None] * n + jnp.einsum("bhl,bhld->bhd", wk, kj)
        return (C_new, n_new, m_new), h

    init = (jnp.zeros((B, H, d, d), jnp.float32), jnp.zeros((B, H, d), jnp.float32), jnp.zeros((B, H), jnp.float32))
    _, hs = lax.scan(step, init, (qc, kc, vc, a, A, li))
    return hs.transpose(1, 0, 3, 2, 4).reshape(B, S, H, d).astype(v.dtype)

def peer_ffn(h, w_pq, sub_keys, u_exp, v_exp):
    B, S, D = h.shape
    T = B * S
    hb = h.reshape(T // PEER_BLOCK, PEER_BLOCK, D)

    def block(xb):
        q = (xb @ w_pq).reshape(PEER_BLOCK, PEER_HEADS, 2, D_KEY // 2)
        s = jnp.einsum("thpd,hpnd->thpn", q, sub_keys).astype(jnp.float32)
        s_top, i_top = lax.top_k(s, PEER_TOPK)
        cand = (s_top[:, :, 0, :, None] + s_top[:, :, 1, None, :]).reshape(PEER_BLOCK, PEER_HEADS, PEER_TOPK * PEER_TOPK)
        best, ci = lax.top_k(cand, PEER_TOPK)
        i1 = jnp.take_along_axis(i_top[:, :, 0, :], ci // PEER_TOPK, axis=-1)
        i2 = jnp.take_along_axis(i_top[:, :, 1, :], ci % PEER_TOPK, axis=-1)
        e = i1 * N_KEYS + i2
        gate = jax.nn.softmax(best, axis=-1)
        u = u_exp[e]
        v = v_exp[e]
        act = jax.nn.gelu(jnp.einsum("thkd,td->thk", u, xb))
        return jnp.einsum("thk,thkd->td", (gate * act).astype(xb.dtype), v)

    return lax.map(block, hb).reshape(B, S, D)

def first_inputs(seed: int = 0) -> dict:
    key = jax.random.key(seed)
    ks = jax.random.split(key, 24)
    nrm = lambda k, shape, s: jax.random.normal(k, shape, jnp.float32) * s
    L = DEPTH
    return {
        "x": nrm(ks[0], (BATCH, SEQ, D_MODEL), 1.0),
        "c": nrm(ks[1], (BATCH, D_MODEL), 1.0),
        "w_ada": nrm(ks[2], (L, D_MODEL, 6 * D_MODEL), 0.5 * D_MODEL ** -0.5),
        "b_ada": nrm(ks[3], (L, 6 * D_MODEL), 0.02),
        "norm1_g": 1.0 + nrm(ks[4], (L, D_MODEL), 0.02),
        "w_in": nrm(ks[5], (L, D_MODEL, IN_COLS), D_MODEL ** -0.5),
        "conv_w": nrm(ks[6], (L, CONV_K, 2 * B_WIDTH), CONV_K ** -0.5),
        "conv_b": nrm(ks[7], (L, 2 * B_WIDTH), 0.02),
        "b_igate": nrm(ks[8], (L, B_HEADS), 0.1),
        "b_fgate": jnp.linspace(3.0, 6.0, B_HEADS)[None, :] + nrm(ks[9], (L, B_HEADS), 0.1),
        "rel_bias": nrm(ks[10], (L, A_HEADS, 2 * REL_CLIP + 1), 0.1),
        "mlstm_norm_g": 1.0 + nrm(ks[11], (L, B_WIDTH), 0.02),
        "w_branch_a": nrm(ks[12], (L, A_WIDTH, D_MODEL), A_WIDTH ** -0.5),
        "w_branch_b": nrm(ks[13], (L, B_WIDTH, D_MODEL), B_WIDTH ** -0.5),
        "w_out": nrm(ks[14], (L, D_MODEL, D_MODEL), D_MODEL ** -0.5),
        "norm2_g": 1.0 + nrm(ks[15], (L, D_MODEL), 0.02),
        "w_peer_q": nrm(ks[16], (L, D_MODEL, PEER_HEADS * D_KEY), D_MODEL ** -0.5),
        "peer_sub_keys": nrm(ks[17], (L, PEER_HEADS, 2, N_KEYS, D_KEY // 2), (D_KEY // 2) ** -0.5),
        "peer_u": nrm(ks[18], (L, N_EXPERTS, D_MODEL), D_MODEL ** -0.5),
        "peer_v": nrm(ks[19], (L, N_EXPERTS, D_MODEL), 0.5),
        "final_g": 1.0 + nrm(ks[20], (D_MODEL,), 0.02),
    }

def first_block(x, c, w_ada, b_ada, norm1_g, w_in, conv_w, conv_b, b_igate, b_fgate, rel_bias, mlstm_norm_g,
              w_branch_a, w_branch_b, w_out, norm2_g, w_peer_q, peer_sub_keys, peer_u, peer_v, final_g):
    B, S, _ = x.shape
    split_at = [int(s) for s in np.cumsum(IN_SIZES)[:-1]]
    for l in range(DEPTH):
        mod = jax.nn.silu(c) @ w_ada[l] + b_ada[l]
        sh1, sc1, gt1, sh2, sc2, gt2 = jnp.split(mod, 6, axis=-1)

        h = modulate(rmsnorm(x, norm1_g[l]), sh1, sc1)
        proj = h @ w_in[l]
        qa, ka, va, qkb, vb, ob, ib, fb, ga, gb = jnp.split(proj, split_at, axis=-1)
        qkb = jax.nn.silu(causal_depthwise_conv(qkb, conv_w[l], conv_b[l]))
        qb, kb = jnp.split(qkb, 2, axis=-1)
        heads_a = lambda t: t.reshape(B, S, A_HEADS, A_HEAD_DIM)
        heads_b = lambda t: t.reshape(B, S, B_HEADS, B_HEAD_DIM)
        y_a = chunk_band_attention(heads_a(qa), heads_a(ka), heads_a(va), rel_bias[l])
        hb = mlstm_chunkwise(heads_b(qb), heads_b(kb), heads_b(vb), ib + b_igate[l], fb + b_fgate[l])
        hb = rmsnorm(hb, mlstm_norm_g[l].reshape(B_HEADS, B_HEAD_DIM)).reshape(B, S, B_WIDTH)
        y_b = jax.nn.sigmoid(ob) * hb
        y = jax.nn.sigmoid(ga) * (y_a @ w_branch_a[l]) + jax.nn.sigmoid(gb) * (y_b @ w_branch_b[l])
        x = x + gt1[:, None, :] * (y @ w_out[l])

        h2 = modulate(rmsnorm(x, norm2_g[l]), sh2, sc2)
        x = x + gt2[:, None, :] * peer_ffn(h2, w_peer_q[l], peer_sub_keys[l], peer_u[l], peer_v[l])
    return rmsnorm(x, final_g)


N_MEM = 256
BLOCK = 128
FOX_HEADS = 8
FOX_HD = 64
SWA_HEADS = 8
SWA_KV_HEADS = 2
SWA_HD = 64
WINDOW = 128
MEM_HEADS = 4
MEM_HD = 128
N_BRANCH = 3
N_EXPERTS_2 = N_KEYS * N_KEYS
PEER_QD = 256
PEER_CHUNK = 128
NEG_INF = -1e30

FOX_W = FOX_HEADS * FOX_HD
SWA_W = SWA_HEADS * SWA_HD
SWA_KV_W = SWA_KV_HEADS * SWA_HD
MEM_W = MEM_HEADS * MEM_HD
IN_WIDTHS = (FOX_W, FOX_W, FOX_W, FOX_HEADS, SWA_W, SWA_KV_W, SWA_KV_W, MEM_W, N_BRANCH * D_MODEL)
IN_COLS_2 = 3 * FOX_W + FOX_HEADS + SWA_W + 2 * SWA_KV_W + MEM_W + N_BRANCH * D_MODEL


def rmsnorm_2(x, g):
    xf = x.astype(jnp.float32)
    y = xf * lax.rsqrt(jnp.mean(xf * xf, axis=-1, keepdims=True) + EPS)
    return (y * g.astype(jnp.float32)).astype(x.dtype)

def head_rmsnorm(x, g):
    xf = x.astype(jnp.float32)
    return xf * lax.rsqrt(jnp.mean(xf * xf, axis=-1, keepdims=True) + EPS) * g.astype(jnp.float32)

def alibi_slopes(n):
    return 2.0 ** (-8.0 * (jnp.arange(n, dtype=jnp.float32) + 1.0) / n)

def fox_attention(q, k, v, log_f):
    B, S, H, d = q.shape
    nb = S // BLOCK
    c = jnp.cumsum(log_f, axis=1).transpose(0, 2, 1)
    q_blocks = q.reshape(B, nb, BLOCK, H, d).transpose(1, 0, 2, 3, 4)
    c_blocks = c.reshape(B, H, nb, BLOCK).transpose(2, 0, 1, 3)
    vf = v.astype(jnp.float32)
    kpos = jnp.arange(S)
    scale = d ** -0.5

    def one_block(args):
        i, q_i, c_i = args
        s = jnp.einsum('bqhd,bkhd->bhqk', q_i, k) * scale
        s = s + (c_i[..., :, None] - c[..., None, :])
        qpos = i * BLOCK + jnp.arange(BLOCK)
        s = jnp.where(kpos[None, :] <= qpos[:, None], s, NEG_INF)
        p = jax.nn.softmax(s, axis=-1)
        return jnp.einsum('bhqk,bkhd->bqhd', p, vf)

    o = lax.map(one_block, (jnp.arange(nb), q_blocks, c_blocks))
    return o.transpose(1, 0, 2, 3, 4).reshape(B, S, H, d)

def swa_attention(q, k, v, sinks, slopes):
    B, S, Hq, d = q.shape
    G = k.shape[2]
    R = Hq // G
    nb = S // BLOCK
    qb = q.reshape(B, nb, BLOCK, G, R, d)

    def band(t):
        t = t.astype(jnp.float32)
        tp = jnp.concatenate([jnp.zeros((B, BLOCK, G, d), jnp.float32), t], axis=1)
        tp = tp.reshape(B, nb + 1, BLOCK, G, d)
        return jnp.concatenate([tp[:, :-1], tp[:, 1:]], axis=2)

    kb = band(k)
    vb = band(v)
    s = jnp.einsum('bnqgrd,bnkgd->bngrqk', qb, kb) * d ** -0.5
    qi = jnp.arange(BLOCK)[:, None]
    kj = jnp.arange(2 * BLOCK)[None, :]
    dist_i = qi + BLOCK - kj
    in_window = (dist_i >= 0) & (dist_i < WINDOW)
    blk_ok = (jnp.arange(nb)[:, None] > 0) | (jnp.arange(2 * BLOCK)[None, :] >= BLOCK)
    mask = in_window[None] & blk_ok[:, None, :]
    s = s - slopes.astype(jnp.float32).reshape(G, R)[:, :, None, None] * dist_i.astype(jnp.float32)
    s = jnp.where(mask[None, :, None, None], s, NEG_INF)
    sink = jnp.broadcast_to(sinks.astype(jnp.float32).reshape(1, 1, G, R, 1, 1), s.shape[:-1] + (1,))
    p = jax.nn.softmax(jnp.concatenate([s, sink], axis=-1), axis=-1)[..., :-1]
    o = jnp.einsum('bngrqk,bnkgd->bnqgrd', p, vb)
    return o.reshape(B, S, Hq, d)

def memory_attention(q, k, v):
    d = q.shape[-1]
    s = jnp.einsum('bshd,bmhd->bhsm', q, k) * d ** -0.5
    p = jax.nn.softmax(s, axis=-1)
    return jnp.einsum('bhsm,bmhd->bshd', p, v.astype(jnp.float32))

def peer_ffn_2(h, w_q, keys1, keys2, u, v):
    B, S, D = h.shape
    half = PEER_QD // 2
    q = (h @ w_q).astype(jnp.float32).reshape(B, S, PEER_HEADS, 2, half)
    s1 = jnp.einsum('bshd,hkd->bshk', q[..., 0, :], keys1.astype(jnp.float32))
    s2 = jnp.einsum('bshd,hkd->bshk', q[..., 1, :], keys2.astype(jnp.float32))
    v1, i1 = lax.top_k(s1, PEER_TOPK)
    v2, i2 = lax.top_k(s2, PEER_TOPK)
    cand = (v1[..., :, None] + v2[..., None, :]).reshape(B, S, PEER_HEADS, PEER_TOPK * PEER_TOPK)
    sv, si = lax.top_k(cand, PEER_TOPK)
    e1 = jnp.take_along_axis(i1, si // PEER_TOPK, axis=-1)
    e2 = jnp.take_along_axis(i2, si % PEER_TOPK, axis=-1)
    experts = e1 * N_KEYS + e2
    gates = jax.nn.softmax(sv, axis=-1)
    n_act = PEER_HEADS * PEER_TOPK
    n_chunks = (B * S) // PEER_CHUNK
    hc = h.reshape(n_chunks, PEER_CHUNK, D)
    ec = experts.reshape(n_chunks, PEER_CHUNK, n_act)
    gc = gates.reshape(n_chunks, PEER_CHUNK, n_act)

    def chunk(args):
        h_c, e_c, g_c = args
        a = jnp.einsum('cd,ced->ce', h_c.astype(jnp.float32), u[e_c].astype(jnp.float32))
        act = jax.nn.gelu(a, approximate=False) * g_c
        return jnp.einsum('ce,ced->cd', act, v[e_c].astype(jnp.float32))

    out = lax.map(chunk, (hc, ec, gc))
    return out.reshape(B, S, D).astype(h.dtype)

def second_inputs(seed: int = 0) -> dict:
    key = jax.random.key(seed)
    ks = jax.random.split(key, 25)
    L = DEPTH
    D = D_MODEL

    def nrm(k, shape, scale):
        return scale * jax.random.normal(k, shape, jnp.float32)

    return {
        'x': nrm(ks[0], (BATCH, SEQ, D), 1.0),
        'mem': nrm(ks[1], (BATCH, N_MEM, D), 1.0),
        'norm1_g': 1.0 + nrm(ks[2], (L, D), 0.02),
        'w_in': nrm(ks[3], (L, D, IN_COLS_2), D ** -0.5),
        'b_gate': nrm(ks[4], (L, N_BRANCH * D), 0.02),
        'b_forget': 2.0 + nrm(ks[5], (L, FOX_HEADS), 0.5),
        'fox_q_g': 1.0 + nrm(ks[6], (L, FOX_HD), 0.02),
        'fox_k_g': 1.0 + nrm(ks[7], (L, FOX_HD), 0.02),
        'swa_q_g': 1.0 + nrm(ks[8], (L, SWA_HD), 0.02),
        'swa_k_g': 1.0 + nrm(ks[9], (L, SWA_HD), 0.02),
        'swa_sinks': nrm(ks[10], (L, SWA_HEADS), 0.5),
        'mem_norm_g': 1.0 + nrm(ks[11], (L, D), 0.02),
        'w_mem_kv': nrm(ks[12], (L, D, 2 * MEM_W), D ** -0.5),
        'mem_q_g': 1.0 + nrm(ks[13], (L, MEM_HD), 0.02),
        'mem_k_g': 1.0 + nrm(ks[14], (L, MEM_HD), 0.02),
        'w_fox_o': nrm(ks[15], (L, FOX_W, D), FOX_W ** -0.5),
        'w_swa_o': nrm(ks[16], (L, SWA_W, D), SWA_W ** -0.5),
        'w_mem_o': nrm(ks[17], (L, MEM_W, D), MEM_W ** -0.5),
        'w_out': nrm(ks[18], (L, D, D), D ** -0.5),
        'norm2_g': 1.0 + nrm(ks[19], (L, D), 0.02),
        'w_peer_q': nrm(ks[20], (L, D, PEER_HEADS * PEER_QD), D ** -0.5),
        'peer_keys1': nrm(ks[21], (L, PEER_HEADS, N_KEYS, PEER_QD // 2), (PEER_QD // 2) ** -0.5),
        'peer_keys2': nrm(ks[22], (L, PEER_HEADS, N_KEYS, PEER_QD // 2), (PEER_QD // 2) ** -0.5),
        'peer_u': nrm(ks[23], (L, N_EXPERTS_2, D), D ** -0.5),
        'peer_v': nrm(ks[24], (L, N_EXPERTS_2, D), (PEER_HEADS * PEER_TOPK) ** -0.5),
    }

def second_block(x, mem, norm1_g, w_in, b_gate, b_forget, fox_q_g, fox_k_g, swa_q_g, swa_k_g,
              swa_sinks, mem_norm_g, w_mem_kv, mem_q_g, mem_k_g, w_fox_o, w_swa_o, w_mem_o,
              w_out, norm2_g, w_peer_q, peer_keys1, peer_keys2, peer_u, peer_v):
    B, S, D = x.shape
    M = mem.shape[1]
    splits = [int(c) for c in np.cumsum(IN_WIDTHS)[:-1]]
    slopes = alibi_slopes(SWA_HEADS)
    for l in range(DEPTH):
        h = rmsnorm_2(x, norm1_g[l])
        z = h @ w_in[l]
        fq, fk, fv, ff, sq, sk, sv, mq, gl = jnp.split(z, splits, axis=-1)

        fq = head_rmsnorm(fq.reshape(B, S, FOX_HEADS, FOX_HD), fox_q_g[l])
        fk = head_rmsnorm(fk.reshape(B, S, FOX_HEADS, FOX_HD), fox_k_g[l])
        log_f = jax.nn.log_sigmoid((ff + b_forget[l]).astype(jnp.float32))
        o_fox = fox_attention(fq, fk, fv.reshape(B, S, FOX_HEADS, FOX_HD), log_f)
        o_fox = o_fox.reshape(B, S, FOX_W).astype(x.dtype)

        sq = head_rmsnorm(sq.reshape(B, S, SWA_HEADS, SWA_HD), swa_q_g[l])
        sk = head_rmsnorm(sk.reshape(B, S, SWA_KV_HEADS, SWA_HD), swa_k_g[l])
        o_swa = swa_attention(sq, sk, sv.reshape(B, S, SWA_KV_HEADS, SWA_HD), swa_sinks[l], slopes)
        o_swa = o_swa.reshape(B, S, SWA_W).astype(x.dtype)

        mn = rmsnorm_2(mem, mem_norm_g[l])
        mk, mv = jnp.split(mn @ w_mem_kv[l], 2, axis=-1)
        mk = head_rmsnorm(mk.reshape(B, M, MEM_HEADS, MEM_HD), mem_k_g[l])
        mq = head_rmsnorm(mq.reshape(B, S, MEM_HEADS, MEM_HD), mem_q_g[l])
        o_mem = memory_attention(mq, mk, mv.reshape(B, M, MEM_HEADS, MEM_HD))
        o_mem = o_mem.reshape(B, S, MEM_W).astype(x.dtype)

        gates = jax.nn.sigmoid((gl + b_gate[l]).astype(jnp.float32)).astype(x.dtype)
        gates = gates.reshape(B, S, N_BRANCH, D)
        merged = (gates[:, :, 0] * (o_fox @ w_fox_o[l])
                  + gates[:, :, 1] * (o_swa @ w_swa_o[l])
                  + gates[:, :, 2] * (o_mem @ w_mem_o[l]))
        x = x + merged @ w_out[l]

        x = x + peer_ffn_2(rmsnorm_2(x, norm2_g[l]), w_peer_q[l], peer_keys1[l], peer_keys2[l],
                         peer_u[l], peer_v[l])
    return x


def setup_inputs(seed=0):
    out = dict(first_inputs(seed))
    for name, value in second_inputs(seed + 1).items():
        if name != "x":
            out[name + "_2"] = value
    return out


def reference(
    x, c, w_ada, b_ada, norm1_g, w_in, conv_w, conv_b, b_igate, b_fgate, rel_bias, mlstm_norm_g,
    w_branch_a, w_branch_b, w_out, norm2_g, w_peer_q, peer_sub_keys, peer_u, peer_v, final_g,
    mem_2, norm1_g_2, w_in_2, b_gate_2, b_forget_2, fox_q_g_2, fox_k_g_2, swa_q_g_2, swa_k_g_2,
    swa_sinks_2, mem_norm_g_2, w_mem_kv_2, mem_q_g_2, mem_k_g_2, w_fox_o_2, w_swa_o_2,
    w_mem_o_2, w_out_2, norm2_g_2, w_peer_q_2, peer_keys1_2, peer_keys2_2, peer_u_2, peer_v_2,
):
    x = first_block(
        x, c, w_ada, b_ada, norm1_g, w_in, conv_w, conv_b, b_igate, b_fgate, rel_bias,
        mlstm_norm_g, w_branch_a, w_branch_b, w_out, norm2_g, w_peer_q, peer_sub_keys, peer_u,
        peer_v, final_g,
    )
    return second_block(
        x, mem_2, norm1_g_2, w_in_2, b_gate_2, b_forget_2, fox_q_g_2, fox_k_g_2, swa_q_g_2,
        swa_k_g_2, swa_sinks_2, mem_norm_g_2, w_mem_kv_2, mem_q_g_2, mem_k_g_2, w_fox_o_2,
        w_swa_o_2, w_mem_o_2, w_out_2, norm2_g_2, w_peer_q_2, peer_keys1_2, peer_keys2_2,
        peer_u_2, peer_v_2,
    )


_drawn_inputs = setup_inputs


def setup_inputs(seed=0):
    import zlib

    import numpy as np

    out = dict(_drawn_inputs(seed))
    spreads = {}
    factors = {'b_ada': 2.776,
     'norm1_g': 8.0,
     'conv_b': 23.943,
     'b_igate': 8.0,
     'rel_bias': 8.0,
     'mlstm_norm_g': 8.0,
     'norm2_g': 4.415,
     'final_g': 2.677,
     'norm1_g_2': 6.047,
     'b_gate_2': 8.0,
     'fox_q_g_2': 8.0,
     'fox_k_g_2': 8.0,
     'swa_q_g_2': 8.0,
     'swa_k_g_2': 8.0,
     'swa_sinks_2': 24.337,
     'mem_norm_g_2': 8.0,
     'mem_q_g_2': 8.0,
     'mem_k_g_2': 8.0,
     'norm2_g_2': 44.221}
    for name, (base, spread) in spreads.items():
        noise = np.random.default_rng([zlib.crc32(name.encode()), seed]).standard_normal(out[name].shape)
        drawn = base * np.exp(spread * noise) if base else spread * noise
        out[name] = jnp.asarray(drawn.astype(out[name].dtype))
    for name, factor in factors.items():
        out[name] = (out[name] * factor).astype(out[name].dtype)
    return out
```

```python
from contextlib import ExitStack

import concourse.bass as bass
from concourse import mybir

F32 = mybir.dt.float32
F32R = mybir.dt.float32r
U32 = mybir.dt.uint32
ALU = mybir.AluOpType
ACT = mybir.ActivationFunctionType
AX = mybir.AxisListType

P = 128
T = 256
QT = T // P
D = 1024
KT = D // P
RAW = 4
RING = 4
GROUP = 4
EXP_BLOCKS = 128
HEADS_P = 8
TOPK = 16
N_KEYS = 128
EPS = 1e-6
NEG = -1e30
CHUNK = 64
MAPS = 4


class Run:

    def __init__(self, name, kind, units):
        self.name, self.kind, self.units = name, kind, units


RUN_LIST = [
    Run("ka_qa", "T", 8), Run("va", "V", 4), Run("qkb", "T", 8), Run("vb", "V", 4),
    Run("gates1", "T", 20), Run("branch_a", "K", 4), Run("branch_b", "K", 4), Run("wout1", "T", 8),
    Run("pq1", "T", 16), Run("u1", "U", 128), Run("v1", "O", 128),
    Run("mk", "T", 4), Run("mv", "V", 4), Run("fq_fk_sq_mq", "T", 16), Run("fv", "V", 4),
    Run("sk", "T", 1), Run("sv", "V", 1), Run("gates2", "T", 24), Run("fox_o", "K", 4),
    Run("swa_o", "K", 4), Run("mem_o", "K", 4), Run("wout2", "T", 8), Run("pq2", "T", 16),
    Run("u2", "U", 128), Run("v2", "O", 128),
]
ADA_UNITS = 48
RUNS = {}


def place_runs():
    unit, half, out = ADA_UNITS, 0, 0
    row = {1: ADA_UNITS, 2: 0}
    block = 1
    for r in RUN_LIST:
        if r.name == "mk":
            block = 2
        r.unit0, r.half0, r.out0, r.block = unit, half, out, block
        if r.kind in "TVK":
            r.row0 = row[block]
            row[block] += r.units
        r.outs = {"T": r.units, "V": r.units, "K": 2 * r.units, "U": r.units, "O": 0}[r.kind]
        unit += r.units
        half += 2 * r.units
        out += r.outs
        RUNS[r.name] = r
    return row


FRONT = place_runs()

COLS = {}


def place_cols():
    at = 0
    for name, n in (("b_ada", 48), ("norm1_g", 8), ("norm2_g", 8), ("final_g", 8), ("conv_b", 8), ("conv_w", 32),
                    ("c", 8), ("mlstm_g", 4), ("norm1_g_2", 8), ("b_gate", 24), ("mem_g", 8), ("norm2_g_2", 8),
                    ("fq_g", 1), ("fk_g", 1), ("sq_g", 1), ("sk_g", 1), ("mq_g", 1), ("mk_g", 1), ("sinks", 8),
                    ("b_i", 1), ("b_f", 1), ("b_forget", 1)):
        COLS[name] = (at, n)
        at += n
    return at


N_COLS = place_cols()

EV = {n: i for i, n in enumerate(["norm1", "branches", "y1", "norm2", "mem", "norm1_2", "fox_swa", "mem_o", "y2",
                                  "norm2_2"])}
NORMS = ["norm1", "norm2", "final", "mem", "norm1_2", "norm2_2"]


def attention_items():
    return ([("a", h) for h in range(8)], [("fox", h) for h in range(8)] + [("swa", h) for h in range(8)]
            + [("mem", h) for h in range(4)])


ITEMS1, ITEMS2 = attention_items()
ITEMS = ITEMS1 + ITEMS2
HEAD_NORMS = [("mk", 0), ("mk", 2), ("mq", 0), ("mq", 2), ("fq", 0), ("fq", 2), ("fk", 0), ("fk", 2),
              ("sq", 0), ("sq", 2), ("sk", 0)]


def two_blocks_kernel(nc, xT_in, memT_in, cols_in, front1, front2, u1, v1, u2, v2, biasA_in, gatew_in, keys_in,
                      out):
    with ExitStack() as ctx:
        def sb(name, shape, dt=F32):
            return ctx.enter_context(nc.sbuf_tensor(name, shape, dt))

        def sem(name):
            return ctx.enter_context(nc.semaphore(name))

        big = sb("big", [P, EXP_BLOCKS * T])
        raw = sb("raw", [P, RAW, KT, P])
        hi = sb("hi", [P, RING, 4, P], F32R)
        lo = sb("lo", [P, RING, 4, P], F32R)
        act_hi = sb("act_hi", [P, KT, T], F32R)
        act_lo = sb("act_lo", [P, KT, T], F32R)
        xT = sb("xT", [P, KT, T])
        scores = sb("scores", [P, QT, 16, N_KEYS])
        chosen = sb("chosen", [P, 3, QT, P])
        ident = sb("ident", [P, P])
        ones = sb("ones", [P, P])
        blockones = sb("blockones", [P, P])
        iota = sb("iota", [P, P])
        zeros = sb("zeros", [P, T])
        cols = sb("cols", [P, N_COLS])
        mod = sb("mod", [P, 48])
        gain = sb("gain", [P, 2, KT])
        small = sb("small", [P, 3, 8])
        neg_sinks = sb("neg_sinks", [P, 8])
        top = sb("top", [P, 2, TOPK])
        topi = sb("topi", [P, 2, TOPK], U32)
        ci = sb("ci", [P, TOPK], U32)
        cpart = sb("cpart", [P, 2, TOPK], U32)
        gsum = sb("gsum", [P, 16])
        eps = sb("eps", [P, 1])
        csilu = sb("csilu", [P, KT])
        g_col = sb("g_col", [P, QT, 8])

        def col(name, i=0):
            at, n = COLS[name]
            return cols[:, at + i:at + i + 1]

        def cut(at, *dims):
            n = 1
            for d in dims:
                n *= d
            v = big[:, at:at + n]
            if len(dims) == 2:
                v = v.rearrange("p (a b) -> p a b", a=dims[0])
            if len(dims) == 3:
                v = v.rearrange("p (a b c) -> p a b c", a=dims[0], b=dims[1])
            return v

        dense = big[:, :].rearrange("p (i t) -> p i t", t=T)
        biasA = cut(0, 8, QT, T)
        kaqa = cut(4096, 8, T)
        va = cut(6144, QT, 512)
        upad = cut(7168, 8, T + 4)
        vb = cut(9248, QT, 512)
        sig1 = cut(10272, 20, T)
        yaT = cut(15392, 4, T)
        qkc = cut(16416, 8, T)
        ybT = cut(18464, 4, T)
        y1 = cut(19488, 8, T)
        tmp = cut(27136, 8, T)
        att_s = cut(27136, 3, QT, T)
        att_pt = cut(30208, 2, QT, T)
        rstd = cut(31232, 2, T)
        keysA = cut(21536, 16, P)
        mls_w = cut(23584, 2, QT, T)
        hb = cut(24608, 4, T)
        rows = cut(25632, 5, T)
        gw = cut(26912, 2, KT, 8)
        peer_q = cut(4096, 16, T)
        biasF = cut(0, 8, QT, T)
        biasS = cut(4096, 8, QT, T)
        heads16 = cut(8192, 16, T)
        skT = cut(12288, 1, T)
        mkT = cut(12544, 4, T)
        fv = cut(13568, QT, 512)
        sv = cut(14592, QT, P)
        mv = cut(14848, QT, 512)
        sig2 = cut(15872, 24, T)
        oT = cut(22016, 12, T)
        y2 = cut(25088, 8, T)
        memT = y2
        dist = cut(22016, QT, T)
        hn_sq = cut(22528, 2, 2 * T)
        hn_r = cut(23552, 2, 2 * T)
        rows2 = cut(31744, 4, T)
        gw2 = cut(24576, KT, 8)
        keysB = cut(0, 16, P)
        peer_q2 = cut(2048, 16, T)

        chosenT = chosen[:, :, :, :].rearrange("p a b c -> p a (b c)")
        flat = scores[:, :, :, :].rearrange("p a b c -> p (a b c)")
        onehot = flat[:, 0:2048].rearrange("p (b t n) -> p b t n", b=MAPS, t=4)
        gatehot = flat[:, 2048:4096].rearrange("p (b t n) -> p b t n", b=MAPS, t=4)

        ps = ctx.enter_context(nc.psum_tensor("ps", [P, 8, 512], F32))
        po = [ps[:, 0, 0:T], ps[:, 1, 0:T]]
        bx = [ps[:, 2 + i, :] for i in range(4)]
        bw = [ps[:, 6, :], ps[:, 7, :]]
        maps = [ps[:, b, :] for b in (6, 7, 0, 1)]
        bo = [ps[:, 5, 0:T], ps[:, 0, 0:T]]
        acc = ps[:, 2:6, :].rearrange("p b (d t) -> p (b d) t", d=2)

        cols_in_s = sem("cols_loaded")
        x_in_s = sem("x_loaded")
        bias_in_s = sem("bias_loaded")
        gw_in_s = [sem("gate_weights_loaded1"), sem("gate_weights_loaded2")]
        keys_in_s = [sem("keys_loaded1"), sem("keys_loaded2")]
        mem_in_s = sem("mem_loaded")
        raw_in = [sem(f"raw_loaded{i}") for i in range(RAW)]
        consts = sem("consts_ready")
        pool_chain = sem("pool_chain")
        dve_chain = sem("dve_chain")
        act_chain = sem("act_chain")
        silu_s = sem("silu_ready")
        ada_used = sem("ada_used")
        mod_s = sem("mod_ready")
        hi_done = sem("hi_done")
        lo_done = sem("lo_done")
        used = sem("halves_used")
        taken = sem("outs_taken")
        n_sq, n_sum, n_rstd = sem("norm_squares"), sem("norm_sums"), sem("norm_rstd")
        n_scaled, n_shifted = sem("norm_scaled"), sem("norm_shifted")
        act_ready = sem("activations_split")
        x_ready = sem("residual_ready")
        att = {n: sem(f"att_{n}") for n in ("s", "m", "e", "p", "t", "c", "o", "y")}
        att_ready = sem("att_bias_ready")
        g_ps, g_row, g_exp, g_ln, g_scan, g_em = (sem(n) for n in (
            "gate_psum", "gate_rows", "gate_exp", "gate_ln", "gate_scan", "gate_em"))
        g_tr, g_col_s = sem("gate_transposed"), sem("gate_cols")
        conv_s, conv_silu = sem("conv_done"), sem("conv_silu")
        m_s, m_d, m_e, m_mask, m_w, m_o, m_h = (sem(f"mlstm_{n}") for n in (
            "scores", "exponents", "weights", "masked", "weighted", "sums", "out"))
        m_sq, m_sum, m_rstd = (sem(f"mlstm_{n}") for n in ("sq", "sum", "rstd"))
        hn = {n: sem(f"headnorm_{n}") for n in ("sq", "sum", "ln", "rstd", "out")}
        fox_bc, fox_d, swa_d = sem("fox_broadcast"), sem("fox_bias"), sem("swa_bias")
        dve_fox = sem("fox_bias_heads")
        sc_ps, sc_taken = sem("scores_psum"), sem("scores_taken")
        top_done, gate_sub, gate_exp, gate_done = (sem(n) for n in (
            "topk_done", "topgate_sub", "topgate_exp", "topgate_done"))
        ch_tr, ch_t = sem("chosen_transposed"), sem("chosen_copied")
        hot_d, hot_sq = sem("one_hot_distances"), sem("one_hot_squares")
        hot_even, hot_odd = sem("one_hots_i1_even"), sem("one_hots_i1_odd")
        hot2, hot_gate = sem("one_hots_i2"), sem("one_hots_gated")
        wmap, w_done = sem("gate_map"), sem("gate_map_applied")
        ahi, alo = sem("dense_hi"), sem("dense_lo")
        out_s = sem("out_stored")

        block = ctx.enter_context(nc.Block())

        def is_static(v):
            return isinstance(v, int)

        def groups(eng, r, body):
            body(0)
            n = r.units // GROUP
            if n > 1:
                with eng.Fori(1, n) as g:
                    body(g)

        @block.sync
        def _(sp):
            def free(n):
                if is_static(n) and n < RAW:
                    return
                if is_static(n) and n < ADA_UNITS + RAW:
                    sp.wait_ge(ada_used, n - RAW + 1)
                else:
                    sp.wait_ge(lo_done, (n - RAW - ADA_UNITS + 1) * 2)

            for n in range(RAW):
                sp.dma_start(raw[:, n, :, :], front1[n]).then_inc(raw_in[n], 16)
            with sp.Fori(1, ADA_UNITS // RAW) as g:
                for j in range(RAW):
                    sp.wait_ge(ada_used, g * RAW + (j - RAW + 1))
                    sp.dma_start(raw[:, j, :, :], front1[bass.ds(g * RAW + j, 1)].rearrange("a p k c -> (a p) k c"))\
                        .then_inc(raw_in[j], 16)

            def source(r, u):
                if r.kind == "U":
                    w = u1 if r.block == 1 else u2
                    return w[bass.ds(u, 1)].rearrange("a p k c -> (a p) k c")
                if r.kind == "O":
                    w = v1 if r.block == 1 else v2
                    return w[:, bass.ds(u, 1), :].rearrange("p a (k c) -> p (a k) c", c=P)
                w = front1 if r.block == 1 else front2
                return w[bass.ds(u + r.row0, 1)].rearrange("a p k c -> (a p) k c")

            for r in RUN_LIST:
                if r.units < GROUP:
                    for u in range(r.units):
                        free(r.unit0 + u)
                        s = (r.unit0 + u) % RAW
                        sp.dma_start(raw[:, s, :, :], source(r, u)).then_inc(raw_in[s], 16)
                    continue

                def body(g, r=r):
                    for j in range(GROUP):
                        u = g * GROUP + j
                        free(u + r.unit0)
                        s = (r.unit0 + j) % RAW
                        sp.dma_start(raw[:, s, :, :], source(r, u)).then_inc(raw_in[s], 16)

                groups(sp, r, body)
            sp.wait_ge(x_ready, 5)
            sp.dma_start(out, xT[:, :, :]).then_inc(out_s, 16)
            sp.wait_ge(out_s, 16)

        @block.gpsimd
        def _(pool):
            n = [0]

            def link(ins):
                n[0] += 1
                ins.then_inc(pool_chain, 1)
                pool.wait_ge(pool_chain, n[0])

            def select(view, pattern, base, mult, fill, op=ALU.is_ge):
                return pool.affine_select(out=view, in_=view, compare_op=op, fill=fill, base=base, pattern=pattern,
                                          channel_multiplier=mult)

            def one_hots(b):
                pool.wait_ge(ch_t, b)

                def body(g):
                    for j in range(1, MAPS, 2):
                        n = g * (MAPS // 2) + (32 * (b - 1) + j // 2)
                        if not is_static(g):
                            pool.wait_ge(wmap, g * MAPS + (64 * (b - 1) + j - MAPS + 1))
                        key = chosenT[:, 0, bass.ds(g * 4 * MAPS + 4 * j, 4)]
                        pool.tensor_tensor(onehot[:, j, :, :], iota[:, :].unsqueeze(1).broadcast_to([P, 4, P]),
                                           key.unsqueeze(2).broadcast_to([P, 4, P]), ALU.subtract)\
                            .then_inc(hot_d, 1)
                        pool.wait_ge(hot_d, n + 1)
                        pool.tensor_tensor(onehot[:, j, :, :], onehot[:, j, :, :], onehot[:, j, :, :], ALU.mult)\
                            .then_inc(hot_sq, 1)

                body(0)
                with pool.Fori(1, 64 // MAPS) as g:
                    body(g)

            link(pool.memset(ones[:, :], 1.0))
            link(pool.memset(zeros[:, :], 0.0))
            link(pool.memset(eps[:, :], EPS))
            link(pool.memset(ident[:, :], 0.0))
            link(select(ident[:, :], [[-1, P]], 0, 1, 1.0, ALU.not_equal))
            link(pool.memset(blockones[:, :], 0.0))
            for b in range(2):
                link(pool.memset(blockones[64 * b:64 * b + 64, 64 * b:64 * b + 64], 1.0))
            link(pool.iota(iota[:, :], pattern=[[1, P]], base=0, channel_multiplier=0,
                           allow_small_or_imprecise_dtypes=True))
            link(pool.memset(upad[:, :, :], 0.0))
            pool.engine_nop().then_inc(consts, 1)
            pool.wait_ge(bias_in_s, 16)
            link(pool.tensor_scalar(biasA, biasA, 8.0, None, ALU.mult))
            for qt in range(QT):
                for half in range(2):
                    limit = CHUNK * (2 * qt + half + 1)
                    v = biasA[64 * half:64 * half + 64, :, qt, :]
                    link(select(v, [[0, 8], [-1, T]], limit - 1, 0, NEG))
            pool.engine_nop().then_inc(att_ready, 1)
            for h in range(4):
                pool.wait_ge(m_e, h + 1)
                select(mls_w[:, h % 2, :, :], [[-P, QT], [1, T]], 0, -1, 0.0).then_inc(m_mask, 1)
            one_hots(1)
            pool.wait_ge(x_ready, 2)
            pool.dma_start(memT, memT_in).then_inc(mem_in_s, 16)
            pool.dma_start(gw2, gatew_in[1]).then_inc(gw_in_s[1], 16)
            link(pool.iota(dist[:, :, :], pattern=[[P, QT], [-1, T]], base=0, channel_multiplier=1,
                           allow_small_or_imprecise_dtypes=True))
            pool.engine_nop().then_inc(swa_d, 1)
            pool.wait_ge(swa_d, 2)
            link(select(biasS, [[0, 8], [P, QT], [-1, T]], 0, 1, NEG))
            link(select(biasS, [[0, 8], [-P, QT], [1, T]], P - 1, -1, NEG))
            pool.wait_ge(fox_d, 1)
            link(select(biasF, [[0, 8], [P, QT], [-1, T]], 0, 1, NEG))
            pool.engine_nop().then_inc(att_ready, 1)
            pool.wait_ge(att["y"], len(ITEMS))
            pool.dma_start(keysB, keys_in[1]).then_inc(keys_in_s[1], 16)
            one_hots(2)

        def item(i):
            kind, h = ITEMS[i]
            o = 64 * (h % 2)
            if kind == "a":
                return dict(q=kaqa[o:o + 64, 4 + h // 2, :], k=kaqa[o:o + 64, h // 2, :], bias=biasA[:, h, :, :],
                            scale=64 ** -0.5, v=lambda kt: va[:, kt, 64 * h:64 * h + 64], dh=64,
                            out=yaT[o:o + 64, h // 2, :], sink=None)
            if kind == "fox":
                return dict(q=heads16[o:o + 64, h // 2, :], k=heads16[o:o + 64, 4 + h // 2, :],
                            bias=biasF[:, h, :, :], scale=64 ** -0.5, v=lambda kt: fv[:, kt, 64 * h:64 * h + 64],
                            dh=64, out=oT[o:o + 64, h // 2, :], sink=None)
            if kind == "swa":
                g = h // 4
                return dict(q=heads16[64 * g:64 * g + 64, 8 + h % 4, :], k=skT[64 * g:64 * g + 64, 0, :],
                            bias=biasS[:, h, :, :], scale=64 ** -0.5, v=lambda kt: sv[:, kt, 64 * g:64 * g + 64],
                            dh=64, out=oT[o:o + 64, 4 + h // 2, :], sink=h)
            return dict(q=heads16[:, 12 + h, :], k=mkT[:, h, :], bias=None, scale=128 ** -0.5,
                        v=lambda kt: mv[:, kt, P * h:P * h + P], dh=P, out=oT[:, 8 + h, :], sink=None)

        def head_norm(i):
            name, u = HEAD_NORMS[i]
            v = {"mk": mkT, "mq": heads16[:, 12:16, :], "fq": heads16[:, 0:4, :], "fk": heads16[:, 4:8, :],
                 "sq": heads16[:, 8:12, :], "sk": skT}[name]
            n = 1 if name == "sk" else 2
            wide = name[0] == "m"
            return v[:, u:u + n, :].rearrange("p a t -> p (a t)"), (ones if wide else blockones), \
                (128 if wide else 64), col(name + "_g"), n * T

        @block.tensor
        def _(pe):
            def norm_sum(name):
                k = NORMS.index(name)
                pe.wait_ge(n_sq, k + 1)
                for kt in range(KT):
                    mm = pe.matmul(bw[0][:, 0:T], ones[:, :], tmp[:, kt, :], start=(kt == 0), stop=(kt == KT - 1))
                mm.then_inc(n_sum, 1)

            def three(out_ap, hi_l, lo_l, hi_r, lo_r, n, first, last, wait_lo, weight_left=True):
                for k in range(n):
                    pe.matmul(out_ap, hi_l(k), hi_r(k), start=(first and k == 0), stop=False, skip_group_check=True)
                for k in range(n):
                    a, b = (hi_l(k), lo_r(k)) if weight_left else (lo_l(k), hi_r(k))
                    pe.matmul(out_ap, a, b, start=False, stop=False, skip_group_check=True)
                wait_lo()
                for k in range(n):
                    a, b = (lo_l(k), hi_r(k)) if weight_left else (hi_l(k), lo_r(k))
                    mm = pe.matmul(out_ap, a, b, start=False, stop=(last and k == n - 1), skip_group_check=True)
                return mm

            def half(r, g, j, h):
                m = (g * GROUP + j) * 2 + (r.half0 + h)
                s = (r.half0 + 2 * j + h) % RING
                pe.wait_ge(hi_done, m + 1)

                def wait_lo():
                    pe.wait_ge(lo_done, m + 1)

                k0 = 4 * h
                if r.kind == "K":
                    o = (r.out0 + 2 * j + h) % 2
                    c0 = 4 if r.name in ("branch_b", "swa_o") else 0
                    mm = three(po[o], lambda k: hi[:, s, k, :], lambda k: lo[:, s, k, :],
                               lambda k: act_hi[:, c0 + k, :], lambda k: act_lo[:, c0 + k, :], 4, True, True, wait_lo)
                elif r.kind in "TU":
                    o = (r.out0 + j) % 2
                    mm = three(po[o], lambda k: hi[:, s, k, :], lambda k: lo[:, s, k, :],
                               lambda k: act_hi[:, k0 + k, :], lambda k: act_lo[:, k0 + k, :], 4, h == 0, h == 1,
                               wait_lo)
                elif r.kind == "V":
                    o = (r.out0 + j) % 2
                    for tt in range(QT):
                        c = slice(P * tt, P * tt + P)
                        mm = three(po[o][:, c], lambda k: act_hi[:, k0 + k, c], lambda k: act_lo[:, k0 + k, c],
                                   lambda k: hi[:, s, k, :], lambda k: lo[:, s, k, :], 4, h == 0 and tt == 0,
                                   h == 1 and tt == 1, wait_lo, weight_left=False)
                else:
                    b = j % 2
                    u = g * GROUP + j
                    base = EXP_BLOCKS * (r.block - 1)
                    if h == 0:
                        pe.wait_ge(ahi, u + (base + 1))
                        pe.wait_ge(alo, u + (base + 1))
                    for k in range(4):
                        for w, a in ((hi, act_hi), (hi, act_lo)):
                            pe.matmul(acc[:, k0 + k, :], w[:, s, k, :], a[:, b, :], start=False, stop=False,
                                      skip_group_check=True)
                    wait_lo()
                    for k in range(4):
                        mm = pe.matmul(acc[:, k0 + k, :], lo[:, s, k, :], act_hi[:, b, :], start=False, stop=False,
                                       skip_group_check=True)
                mm.then_inc(used, 1)

            def outs_free(r, o):
                if is_static(o) and o < 2:
                    return
                pe.wait_ge(taken, o - 1)

            def run(name, loop=True):
                r = RUNS[name]
                if r.kind != "O" and r.out0:
                    pe.wait_ge(taken, r.out0)

                def body(g):
                    for j in range(min(GROUP, r.units)):
                        for h in range(2):
                            if r.kind == "K":
                                outs_free(r, (g * GROUP + j) * 2 + (r.out0 + h))
                            elif h == 0 and r.kind != "O":
                                outs_free(r, g * GROUP + (r.out0 + j))
                            half(r, g, j, h)

                if r.units < GROUP:
                    body(0)
                else:
                    groups(pe, r, body)

            def transpose(out_ap, in_ap, n):
                return pe.transpose(out_ap, in_ap, ident[0:n, 0:n])

            def attention(first, last):
                def s(i):
                    a = item(i)
                    if i >= 2:
                        pe.wait_ge(att["m"], i - 1)
                    for qt in range(QT):
                        mm = pe.matmul(bx[i % 2][:, qt * T:qt * T + T], a["q"][:, P * qt:P * qt + P], a["k"],
                                       start=True, stop=True)
                    mm.then_inc(att["s"], 1)

                def pt(i):
                    pe.wait_ge(att["p"], i + 1)
                    if i >= 1:
                        pe.wait_ge(att["c"], i)
                    for kt in range(QT):
                        for qt in range(QT):
                            mm = pe.transpose(bx[2][:, kt * T + qt * P:kt * T + qt * P + P],
                                              att_s[:, i % 3, qt, kt * P:kt * P + P], ident[:, :])
                    mm.then_inc(att["t"], 1)

                def o(i):
                    a = item(i)
                    pe.wait_ge(att["c"], i + 1)
                    if i >= 2:
                        pe.wait_ge(att["y"], i - 1)
                    for kt in range(QT):
                        mm = pe.matmul(bo[i % 2][0:a["dh"], :], a["v"](kt),
                                       att_pt[:, i % 2, kt, :], start=(kt == 0), stop=(kt == QT - 1))
                    mm.then_inc(att["o"], 1)

                s(first)
                s(first + 1)
                for i in range(first, last):
                    if i + 2 < last:
                        s(i + 2)
                    if i > first:
                        o(i - 1)
                    pt(i)
                o(last - 1)

            def broadcast_row(out_ap, rows_ap, n, h):
                return pe.matmul(out_ap, ident[0:n, h:h + 1].broadcast_to([n, P]), rows_ap, start=True, stop=True)

            def peer_scores(b, q, keys):
                pe.wait_ge(keys_in_s[b - 1], 16)
                pe.wait_ge(taken, RUNS[f"pq{b}"].out0 + 16)
                for c in range(8):
                    n = 8 * (b - 1) + c
                    if n >= 2:
                        pe.wait_ge(sc_taken, n - 1)
                    tt, p0 = c // 4, 4 * (c % 4)
                    for k in range(4):
                        mm = pe.matmul(bw[c % 2][:, k * P:k * P + P], q[:, p0 + k, tt * P:tt * P + P],
                                       keys[:, p0 + k, :], start=True, stop=True)
                    mm.then_inc(sc_ps, 1)

            def gate_map(b):
                pe.wait_ge(gate_done, b)
                for c in range(3):
                    for tt in range(QT):
                        mm = pe.transpose(bx[c][:, tt * P:tt * P + P], chosen[:, c, tt, :], ident[:, :])
                mm.then_inc(ch_tr, 1)

                def body(g):
                    for j in range(MAPS):
                        n = g * MAPS + (64 * (b - 1) + j)
                        pe.wait_ge(hot_odd if j % 2 else hot_even, g * (MAPS // 2) + (32 * (b - 1) + j // 2 + 1))
                        pe.wait_ge(hot_gate, n + 1)
                        if not is_static(n) or n >= MAPS:
                            pe.wait_ge(w_done, n - MAPS + 1)
                        for t in range(4):
                            mm = pe.matmul(maps[j][:, t * P:t * P + P], onehot[:, j, t, :], gatehot[:, j, t, :],
                                           start=True, stop=True)
                        mm.then_inc(wmap, 1)

                body(0)
                with pe.Fori(1, 64 // MAPS) as g:
                    body(g)

            def experts(b):
                peer_scores(b, peer_q if b == 1 else peer_q2, keysA if b == 1 else keysB)
                pe.wait_ge(act_ready, 2 * EV["norm2" if b == 1 else "norm2_2"] + 2)
                run(f"u{b}")
                gate_map(b)
                pe.wait_ge(ch_t, b)
                for d in range(KT):
                    pe.matmul(acc[:, d, :], zeros[:, 0:P], zeros[:, :], start=(d % 2 == 0), stop=False,
                              skip_group_check=True)
                run(f"v{b}")

            pe.wait_ge(consts, 1)
            pe.wait_ge(silu_s, 1)

            for u in range(ADA_UNITS):
                pe.wait_ge(raw_in[u % RAW], 16 * (u // RAW + 1))
                for kt in range(KT):
                    mm = pe.matmul(bw[1][:, u:u + 1], raw[:, u % RAW, kt, :], csilu[:, kt:kt + 1],
                                   start=(kt == 0), stop=(kt == KT - 1))
                mm.then_inc(ada_used, 1)
            norm_sum("norm1")
            pe.wait_ge(act_ready, 2 * EV["norm1"] + 2)
            run("ka_qa")
            pe.wait_ge(gw_in_s[0], 16)
            pe.wait_ge(mod_s, 1)
            for c in range(2):
                for kt in range(KT):
                    mm = pe.matmul(bw[c][0:4, 0:T], gw[:, 0, kt, 4 * c:4 * c + 4], tmp[:, kt, :],
                                   start=(kt == 0), stop=(kt == KT - 1))
            mm.then_inc(g_ps, 1)
            for name in ("va", "qkb", "vb", "gates1"):
                run(name)
            pe.wait_ge(taken, RUNS["gates1"].out0 + 20)
            pe.wait_ge(att_ready, 1)
            attention(0, len(ITEMS1))
            pe.wait_ge(g_scan, 1)
            for tt in range(QT):
                mm = transpose(bw[0][:, 8 * tt:8 * tt + 4], rows[0:4, 0, tt * P:tt * P + P], 4)
            mm.then_inc(g_tr, 1)
            pe.wait_ge(g_em, 1)
            pe.wait_ge(g_col_s, 1)
            pe.wait_ge(conv_silu, 1)
            pe.wait_ge(att["y"], len(ITEMS1))

            def mlstm_scores(h):
                if h >= 2:
                    pe.wait_ge(m_w, h - 1)
                    pe.wait_ge(m_h, h - 1)
                for st in range(QT):
                    pe.matmul(bx[h % 2][:, st * T:st * T + T], qkc[:, 4 + h, st * P:st * P + P], qkc[:, h, :],
                              start=True, stop=True)
                broadcast_row(bw[h % 2][:, 0:T], rows[0:4, 1, :], 4, h)
                broadcast_row(bw[h % 2][:, T:2 * T], rows[0:4, 2, :], 4, h).then_inc(m_s, 1)

            def mlstm_sums(h):
                pe.wait_ge(m_w, h + 1)
                o = bx[2 + h % 2]
                for st in range(QT):
                    pe.matmul(o[:, 0:T], vb[:, st, h * P:h * P + P], mls_w[:, h % 2, st, :], start=(st == 0),
                              stop=(st == 1))
                for st in range(QT):
                    mm = pe.matmul(o[:, T:2 * T], ones[:, :], mls_w[:, h % 2, st, :], start=(st == 0),
                                   stop=(st == 1))
                mm.then_inc(m_o, 1)

            mlstm_scores(0)
            for h in range(4):
                if h < 3:
                    mlstm_scores(h + 1)
                mlstm_sums(h)
            pe.wait_ge(m_sq, 1)
            for h in range(4):
                mm = pe.matmul(bx[h // 2][:, (h % 2) * T:(h % 2) * T + T], ones[:, :], tmp[:, h, :], start=True,
                               stop=True)
            mm.then_inc(m_sum, 1)
            pe.wait_ge(act_ready, 2 * EV["branches"] + 2)
            run("branch_a")
            run("branch_b")
            pe.wait_ge(act_ready, 2 * EV["y1"] + 2)
            run("wout1")
            norm_sum("norm2")
            pe.wait_ge(act_ready, 2 * EV["norm2"] + 2)
            run("pq1")
            experts(1)
            norm_sum("final")
            norm_sum("mem")
            pe.wait_ge(act_ready, 2 * EV["mem"] + 2)
            run("mk")
            run("mv")
            norm_sum("norm1_2")
            pe.wait_ge(act_ready, 2 * EV["norm1_2"] + 2)
            pe.wait_ge(gw_in_s[1], 16)
            for kt in range(KT):
                mm = pe.matmul(bw[0][0:8, 0:T], gw2[:, kt, :], tmp[:, kt, :], start=(kt == 0), stop=(kt == KT - 1))
            mm.then_inc(g_ps, 1)
            run("fq_fk_sq_mq")
            run("fv")
            run("sk")
            run("sv")
            run("gates2")
            pe.wait_ge(g_scan, 2)
            for tt in range(QT):
                mm = transpose(bw[0][:, 8 * tt:8 * tt + 8], rows2[0:8, 2, tt * P:tt * P + P], 8)
            mm.then_inc(g_tr, 1)
            pe.wait_ge(g_col_s, 2)
            for h in range(8):
                if h >= 2:
                    pe.wait_ge(dve_fox, h - 1)
                broadcast_row(bw[h % 2][:, 0:T], rows2[0:8, 2, :], 8, h).then_inc(fox_bc, 1)
            for i in range(len(HEAD_NORMS)):
                src, mat, d, g, n = head_norm(i)
                pe.wait_ge(hn["sq"], i + 1)
                if i < 2:
                    pe.wait_ge(dve_fox, 8)
                else:
                    pe.wait_ge(hn["ln"], i - 1)
                pe.matmul(bw[i % 2][:, 0:n], mat[:, :], hn_sq[:, i % 2, 0:n], start=True, stop=True)\
                    .then_inc(hn["sum"], 1)
            pe.wait_ge(hn["out"], len(HEAD_NORMS))
            pe.wait_ge(att_ready, 2)
            attention(len(ITEMS1), len(ITEMS))
            pe.wait_ge(act_ready, 2 * EV["fox_swa"] + 2)
            run("fox_o")
            run("swa_o")
            pe.wait_ge(act_ready, 2 * EV["mem_o"] + 2)
            run("mem_o")
            pe.wait_ge(act_ready, 2 * EV["y2"] + 2)
            run("wout2")
            norm_sum("norm2_2")
            pe.wait_ge(act_ready, 2 * EV["norm2_2"] + 2)
            run("pq2")
            experts(2)

        @block.scalar
        def _(act):
            n_chain = [0]

            def link(ins):
                n_chain[0] += 1
                ins.then_inc(act_chain, 1)
                act.wait_ge(act_chain, n_chain[0])

            act.dma_start(cols[:, :], cols_in).then_inc(cols_in_s, 16)
            act.dma_start(xT[:, :, :], xT_in).then_inc(x_in_s, 16)
            act.dma_start(gw, gatew_in.rearrange("b p k c -> p b k c")).then_inc(gw_in_s[0], 16)
            act.dma_start(biasA, biasA_in).then_inc(bias_in_s, 16)
            act.dma_start(keysA, keys_in[0]).then_inc(keys_in_s[0], 16)

            def weight_hi(r, g, j, h):
                m = (g * GROUP + j) * 2 + (r.half0 + h)
                s = (r.half0 + 2 * j + h) % RING
                rs = (r.unit0 + j) % RAW
                if h == 0:
                    act.wait_ge(raw_in[rs], g * 16 + 16 * ((r.unit0 + j) // RAW + 1))
                if not (is_static(m) and m < RING):
                    act.wait_ge(used, m - RING + 1)
                act.activation(hi[:, s, :, :], raw[:, rs, 4 * h:4 * h + 4, :], ACT.Copy).then_inc(hi_done, 1)

            def run(name, evict=None):
                r = RUNS[name]

                def body(g):
                    for j in range(min(GROUP, r.units)):
                        for h in range(2):
                            weight_hi(r, g, j, h)
                        if evict and not (j == 0 and is_static(g) and g == 0):
                            out(g * GROUP + (j - 1), (r.out0 + j - 1) % 2)

                def out(u, b):
                    act.wait_ge(used, u * 2 + (r.half0 + 2))
                    evict(u, po[b]).then_inc(taken, 1)

                if r.units < GROUP:
                    body(0)
                else:
                    groups(act, r, body)
                if evict:
                    out(r.units - 1, (r.out0 + r.units - 1) % 2)

            def to(dst, func=ACT.Copy):
                return lambda u, p: act.activation(dst[:, bass.ds(u, 1), :].rearrange("p a t -> p (a t)"), p, func)

            def to_tokens(dst):
                return lambda u, p: act.activation(dst[:, :, u * P:u * P + P],
                                                   p.rearrange("p (a c) -> p a c", a=QT), ACT.Copy)

            def run_v(name, dst):
                run(name, to_tokens(dst))

            def norm_squares(name, src):
                act.activation(tmp, src, ACT.Square).then_inc(n_sq, 1)
                act.wait_ge(n_sum, NORMS.index(name) + 1)
                if name == "mem":
                    act.wait_ge(x_ready, 3)
                link(act.activation(rstd[:, 0, :], bw[0][:, 0:T], ACT.Ln, bias=eps[:, :], scale=1.0 / D))
                act.activation(rstd[:, 1, :], rstd[:, 0, :], ACT.Exp, scale=-0.5).then_inc(n_rstd, 1)

            def norm_shift(k, at):
                for kt in range(KT):
                    act.wait_ge(n_scaled, 8 * k + kt + 1)
                    act.activation(tmp[:, kt, :], tmp[:, kt, :], ACT.Identity, bias=mod[:, at + kt:at + kt + 1])\
                        .then_inc(n_shifted, 1)

            def attention(first, last):
                def exps(i):
                    a = item(i)
                    act.wait_ge(att["m"], i + 1)
                    sm = small[:, i % 3, :]
                    if a["sink"] is not None:
                        for qt in range(QT):
                            act.activation(sm[:, 4 + qt:5 + qt], col("sinks", a["sink"]), ACT.Exp,
                                           bias=sm[:, qt:qt + 1])
                    for qt in range(QT):
                        ins = act.activation(att_s[:, i % 3, qt, :], att_s[:, i % 3, qt, :], ACT.Exp,
                                             bias=sm[:, qt:qt + 1], scale=-1.0, accum_out=sm[:, 2 + qt:3 + qt])
                    ins.then_inc(att["e"], 1)

                def copy(i):
                    act.wait_ge(att["t"], i + 1)
                    if i >= 2:
                        act.wait_ge(att["o"], i - 1)
                    act.activation(att_pt[:, i % 2, :, :].rearrange("p a t -> p (a t)"), bx[2], ACT.Copy)\
                        .then_inc(att["c"], 1)

                exps(first)
                exps(first + 1)
                for i in range(first, last):
                    if i + 2 < last:
                        exps(i + 2)
                    copy(i)

            def log_gate(k, r):
                act.wait_ge(g_row, k + 1)
                act.activation(r, r, ACT.Exp, scale=-1.0).then_inc(g_exp, 1)
                act.wait_ge(g_exp, 2 * k + 2)
                act.activation(r, r, ACT.Ln).then_inc(g_ln, 1)

            def experts(b):
                for c in range(8):
                    act.wait_ge(sc_ps, 8 * (b - 1) + c + 1)
                    act.activation(scores[:, c // 4, 4 * (c % 4):4 * (c % 4) + 4, :].rearrange("p a n -> p (a n)"),
                                   bw[c % 2], ACT.Copy).then_inc(sc_taken, 1)
                act.preload_act_table(ACT.Gelu_apprx_tanh if b == 1 else ACT.Gelu)
                run(f"u{b}", to(dense, ACT.Gelu_apprx_tanh if b == 1 else ACT.Gelu))
                act.wait_ge(gate_sub, b)
                g = chosen[:, 2, :, :].rearrange("p a b -> p (a b)")
                act.activation(g, g, ACT.Exp).then_inc(gate_exp, 1)
                act.wait_ge(ch_t, b)

                def gate_hots(g):
                    for j in range(MAPS):
                        if j % 2:
                            act.wait_ge(hot_sq, g * (MAPS // 2) + (32 * (b - 1) + j // 2 + 1))
                            act.activation(onehot[:, j, :, :], onehot[:, j, :, :], ACT.Relu, bias=ones[:, 0:1],
                                           scale=-1.0).then_inc(hot_odd, 1)
                        act.wait_ge(hot2, g * MAPS + (64 * (b - 1) + j + 1))
                        for t in range(4):
                            tok = g * 4 * MAPS + (4 * j + t)
                            ins = act.activation(gatehot[:, j, t, :], gatehot[:, j, t, :], ACT.Copy,
                                                 scale=chosenT[:, 2, bass.ds(tok, 1)])
                        ins.then_inc(hot_gate, 1)

                gate_hots(0)
                with act.Fori(1, 64 // MAPS) as g:
                    gate_hots(g)
                r = RUNS[f"v{b}"]
                act.wait_ge(w_done, 64 * b)

                def body(g):
                    for j in range(GROUP):
                        u = g * GROUP + j
                        base = EXP_BLOCKS * (b - 1)
                        if is_static(g) and g == 0 and j < 2:
                            act.wait_ge(used, r.half0)
                        else:
                            act.wait_ge(used, u * 2 + (r.half0 - 2))
                        act.activation(act_hi[:, j % 2, :], dense[:, bass.ds(u, 1), :].rearrange("p a t -> p (a t)"),
                                       ACT.Copy).then_inc(ahi, 1)
                        for h in range(2):
                            weight_hi(r, g, j, h)

                groups(act, r, body)

            act.wait_ge(cols_in_s, 16)
            act.activation(csilu[:, :], cols[:, COLS["c"][0]:COLS["c"][0] + 8], ACT.Silu).then_inc(silu_s, 1)
            act.wait_ge(x_in_s, 16)
            act.wait_ge(consts, 1)
            norm_squares("norm1", xT[:, :, :])
            norm_shift(0, 0)
            act.preload_act_table(ACT.Copy)
            run("ka_qa", to(kaqa))
            run_v("va", va)
            run("qkb", lambda u, p: act.activation(
                upad[:, bass.ds(u, 1), 4:4 + T].rearrange("p a t -> p (a t)"), p, ACT.Copy))
            run_v("vb", vb)
            act.preload_act_table(ACT.Sigmoid)
            run("gates1", to(sig1, ACT.Sigmoid))
            log_gate(0, rows[0:4, 2, :])
            act.wait_ge(g_scan, 1)
            act.activation(rows[0:4, 2, :], rows[0:4, 2, :], ACT.Exp, scale=-1.0).then_inc(g_em, 1)
            act.wait_ge(conv_s, 1)
            act.activation(qkc, qkc, ACT.Silu).then_inc(conv_silu, 1)
            attention(0, len(ITEMS1))
            for h in range(4):
                act.wait_ge(m_d, h + 1)
                w = mls_w[:, h % 2, :, :]
                act.activation(w, w, ACT.Exp, scale=-1.0).then_inc(m_e, 1)
            act.wait_ge(m_h, 4)
            act.activation(tmp[:, 0:4, :], hb, ACT.Square).then_inc(m_sq, 1)
            act.wait_ge(m_sum, 1)
            for c in range(2):
                ins = act.activation(tmp[:, 2 * c:2 * c + 2, :].rearrange("p a t -> p (a t)"), bx[c], ACT.Ln,
                                     bias=eps[:, :], scale=1.0 / P)
            link(ins)
            act.activation(tmp[:, 4:8, :], tmp[:, 0:4, :], ACT.Exp, scale=-0.5).then_inc(m_rstd, 1)
            run("branch_a")
            run("branch_b")
            run("wout1")
            act.wait_ge(x_ready, 1)
            norm_squares("norm2", xT[:, :, :])
            norm_shift(1, 24)
            run("pq1", to(peer_q))
            experts(1)
            act.wait_ge(x_ready, 2)
            norm_squares("final", xT[:, :, :])
            act.wait_ge(mem_in_s, 16)
            norm_squares("mem", memT)
            run("mk", to(mkT))
            run_v("mv", mv)
            act.wait_ge(x_ready, 3)
            act.wait_ge(act_ready, 2 * EV["mem"] + 2)
            norm_squares("norm1_2", xT[:, :, :])
            act.preload_act_table(ACT.Copy)
            run("fq_fk_sq_mq", to(heads16))
            run_v("fv", fv)
            run("sk", to(skT))
            run_v("sv", sv)
            act.preload_act_table(ACT.Sigmoid)
            run("gates2", lambda u, p: act.activation(
                sig2[:, bass.ds(u, 1), :].rearrange("p a t -> p (a t)"), p, ACT.Sigmoid,
                bias=cols[:, bass.ds(COLS["b_gate"][0] + u, 1)]))
            log_gate(1, rows2[0:8, 1, :])

            def hn_square(i):
                src, mat, d, g, n = head_norm(i)
                if i >= 2:
                    act.wait_ge(hn["sum"], i - 1)
                act.activation(hn_sq[:, i % 2, 0:n], src, ACT.Square).then_inc(hn["sq"], 1)

            act.wait_ge(taken, RUNS["gates2"].out0 + 24)
            hn_square(0)
            for i in range(len(HEAD_NORMS)):
                if i + 1 < len(HEAD_NORMS):
                    hn_square(i + 1)
                src, mat, d, g, n = head_norm(i)
                r = hn_r[:, i % 2, 0:n]
                act.wait_ge(hn["sum"], i + 1)
                if i >= 2:
                    act.wait_ge(hn["out"], i - 1)
                ins = act.activation(r, bw[i % 2][:, 0:n], ACT.Ln, bias=eps[:, :], scale=1.0 / d)
                ins.then_inc(hn["ln"], 1)
                act.wait_ge(hn["ln"], i + 1)
                act.activation(r, r, ACT.Exp, scale=-0.5).then_inc(hn["rstd"], 1)
            attention(len(ITEMS1), len(ITEMS))
            for name in ("fox_o", "swa_o", "mem_o", "wout2"):
                run(name)
            act.wait_ge(x_ready, 4)
            norm_squares("norm2_2", xT[:, :, :])
            run("pq2", to(peer_q2))
            experts(2)

        @block.vector
        def _(dve):
            n_chain = [0]

            def link(ins):
                n_chain[0] += 1
                ins.then_inc(dve_chain, 1)
                dve.wait_ge(dve_chain, n_chain[0])

            def weight_lo(r, g, j, h):
                m = (g * GROUP + j) * 2 + (r.half0 + h)
                s = (r.half0 + 2 * j + h) % RING
                rs = (r.unit0 + j) % RAW
                dve.wait_ge(hi_done, m + 1)
                dve.tensor_tensor(lo[:, s, :, :], raw[:, rs, 4 * h:4 * h + 4, :], hi[:, s, :, :].bitcast(F32),
                                  ALU.subtract).then_inc(lo_done, 1)

            def run(name, evict=None):
                r = RUNS[name]
                per = 2 if r.kind == "K" else 1

                def out(u, b):
                    dve.wait_ge(used, (u * 2 // per) + (r.half0 + 2 // per) if is_static(u) else
                                u * (2 // per) + (r.half0 + 2 // per))
                    evict(u, po[b]).then_inc(taken, 1)

                def body(g):
                    for j in range(min(GROUP, r.units)):
                        for h in range(2):
                            weight_lo(r, g, j, h)
                            if evict and per == 2 and not (is_static(g) and g == 0 and j == 0 and h == 0):
                                out(g * GROUP * 2 + (2 * j + h - 1), (r.out0 + 2 * j + h - 1) % 2)
                        if evict and per == 1 and not (is_static(g) and g == 0 and j == 0):
                            out(g * GROUP + (j - 1), (r.out0 + j - 1) % 2)

                if r.units < GROUP:
                    body(0)
                else:
                    groups(dve, r, body)
                if evict:
                    out(r.outs - 1, (r.out0 + r.outs - 1) % 2)

            def split_ready(event, *parts):
                for i, (c, src) in enumerate(parts):
                    n = src.shape[1]
                    link(dve.tensor_copy(act_hi[:, c:c + n, :], src))
                    ins = dve.tensor_tensor(act_lo[:, c:c + n, :], src, act_hi[:, c:c + n, :].bitcast(F32),
                                            ALU.subtract)
                    if i == len(parts) - 1:
                        ins.then_inc(act_ready, 2)

            def norm_apply(name, src, gains, shift_k=None, used_before=None):
                dve.wait_ge(n_rstd, NORMS.index(name) + 1)
                for kt in range(KT):
                    dve.scalar_tensor_tensor(out=tmp[:, kt, :], in0=src[:, kt, :], scalar=gains(kt),
                                             in1=rstd[:, 1, :], op0=ALU.mult, op1=ALU.mult).then_inc(n_scaled, 1)
                dve.wait_ge(n_scaled, n_scaled_at[name])
                if shift_k is not None:
                    dve.wait_ge(n_shifted, 8 * (shift_k + 1))
                if used_before is not None:
                    dve.wait_ge(used, used_before)
                split_ready(EV[name], (0, tmp))

            n_scaled_at = {"norm1": 8, "norm2": 16, "mem": 24, "norm1_2": 32, "norm2_2": 40}

            def attention(first, last):
                def bias_max(i):
                    a = item(i)
                    dve.wait_ge(att["s"], i + 1)
                    if i >= 3:
                        dve.wait_ge(att["t"], i - 2)
                    for qt in range(QT):
                        bias = zeros[:, :] if a["bias"] is None else a["bias"][:, qt, :]
                        start = 3e38 if a["sink"] is None else neg_sinks[:, a["sink"]:a["sink"] + 1]
                        ins = dve.tensor_tensor_reduce(out=att_s[:, i % 3, qt, :], in0=bx[i % 2][:, qt * T:qt * T + T],
                                                       in1=bias, scale=-a["scale"], scalar=start, op0=ALU.add,
                                                       op1=ALU.min, accum_out=small[:, i % 3, qt:qt + 1])
                    ins.then_inc(att["m"], 1)

                def normalise(i):
                    a = item(i)
                    dve.wait_ge(att["e"], i + 1)
                    sm = small[:, i % 3, :]
                    if a["sink"] is not None:
                        link(dve.tensor_tensor(sm[:, 2:4], sm[:, 2:4], sm[:, 4:6], ALU.add))
                    link(dve.reciprocal(sm[:, 6:8], sm[:, 2:4]))
                    for qt in range(QT):
                        ins = dve.tensor_scalar(att_s[:, i % 3, qt, :], att_s[:, i % 3, qt, :], sm[:, 6 + qt:7 + qt],
                                                None, ALU.mult)
                    ins.then_inc(att["p"], 1)

                def take(i):
                    a = item(i)
                    dve.wait_ge(att["o"], i + 1)
                    dve.tensor_copy(a["out"], bo[i % 2][0:a["dh"], :]).then_inc(att["y"], 1)

                bias_max(first)
                bias_max(first + 1)
                for i in range(first, last):
                    normalise(i)
                    if i + 2 < last:
                        bias_max(i + 2)
                    if i > first:
                        take(i - 1)
                take(last - 1)

            def log_sigmoid(k, n, f_ps, bias, r):
                link(dve.tensor_scalar(r(0), f_ps, bias, None, ALU.add))
                link(dve.scalar_tensor_tensor(out=r(1), in0=r(0), scalar=-1.0, in1=r(0), op0=ALU.mult, op1=ALU.max))
                dve.tensor_scalar(r(0), r(0), 0.0, None, ALU.min).then_inc(g_row, 1)
                dve.wait_ge(g_exp, 2 * k + 1)
                dve.tensor_scalar(r(1), r(1), 1.0, None, ALU.add).then_inc(g_exp, 1)
                dve.wait_ge(g_ln, k + 1)
                link(dve.tensor_tensor(r(0), r(0), r(1), ALU.subtract))

            def topk_scores(tt, pair):
                s = scores[:, tt, pair, :]
                p = pair % 2
                for half in range(2):
                    c = slice(8 * half, 8 * half + 8)
                    link(dve.max(top[:, p, c], s))
                    link(dve.max_index(topi[:, p, c], top[:, p, c], s))
                    if half == 0:
                        link(dve.match_replace(s, top[:, p, c], s, -3e38))

            cand = bw[0][:, 0:T].rearrange("p (a b) -> p a b", a=TOPK)
            same = bw[1][:, 0:T].rearrange("p (a b) -> p a b", a=TOPK)

            def topk_pairs(tt, h):
                link(dve.tensor_tensor(cand, top[:, 0, :].unsqueeze(2).broadcast_to([P, TOPK, TOPK]),
                                       top[:, 1, :].unsqueeze(1).broadcast_to([P, TOPK, TOPK]), ALU.add))
                flat_c = bw[0][:, 0:T]
                best = chosen[:, 2, tt, TOPK * h:TOPK * h + TOPK]
                for half in range(2):
                    c = slice(8 * half, 8 * half + 8)
                    link(dve.max(best[:, c], flat_c))
                    link(dve.max_index(ci[:, c], best[:, c], flat_c))
                    if half == 0:
                        link(dve.match_replace(flat_c, best[:, c], flat_c, -3e38))

            def topk_experts(tt, h):
                link(dve.tensor_scalar(cpart[:, 0, :], ci[:, :], 4, None, ALU.logical_shift_right))
                link(dve.tensor_scalar(cpart[:, 1, :], ci[:, :], 15, None, ALU.bitwise_and))
                for p in range(2):
                    rank = cpart[:, p, :].unsqueeze(2).broadcast_to([P, TOPK, TOPK])
                    key = topi[:, p, :].unsqueeze(1).broadcast_to([P, TOPK, TOPK])
                    link(dve.tensor_tensor(same, rank, iota[:, 0:TOPK].unsqueeze(1).broadcast_to([P, TOPK, TOPK]),
                                           ALU.is_equal))
                    link(dve.tensor_tensor(same, same, key, ALU.mult))
                    link(dve.tensor_reduce(chosen[:, p, tt, TOPK * h:TOPK * h + TOPK], same, AX.X, ALU.add))

            def experts(b):
                r = RUNS[f"u{b}"]
                dve.wait_ge(sc_taken, 8 * b)
                step = 0
                for u in range(r.units):
                    for h in range(2):
                        weight_lo_static(r, u, h)
                    if u >= 4 and u % 7 in (0, 1, 3, 5) and step < 64:
                        tt, rest = step // 32, step % 32
                        head, part = rest // 4, rest % 4
                        if part < 2:
                            topk_scores(tt, 2 * head + part)
                        elif part == 2:
                            topk_pairs(tt, head)
                        else:
                            topk_experts(tt, head)
                        step += 1
                assert step == 64
                g = chosen[:, 2, :, :].rearrange("p a (h k) -> p (a h) k", k=TOPK)
                link(dve.tensor_copy(gsum[:, :], g[:, :, 0:1].rearrange("p a k -> p (a k)")))
                dve.tensor_tensor(g, g, gsum[:, :].unsqueeze(2).broadcast_to([P, 16, TOPK]), ALU.subtract)\
                    .then_inc(gate_sub, 1)
                dve.wait_ge(gate_exp, b)
                link(dve.tensor_reduce(gsum[:, :], g, AX.X, ALU.add))
                link(dve.reciprocal(gsum[:, :], gsum[:, :]))
                dve.tensor_tensor(g, g, gsum[:, :].unsqueeze(2).broadcast_to([P, 16, TOPK]), ALU.mult)\
                    .then_inc(gate_done, 1)
                dve.wait_ge(ch_tr, b)
                for c in range(3):
                    ins = dve.tensor_copy(chosenT[:, c, :], bx[c][:, 0:T])
                link(ins)
                dve.engine_nop().then_inc(ch_t, 1)
                dve.wait_ge(taken, r.out0 + r.outs)

                def hots(g, j):
                    if j % 2 == 0:
                        key = chosenT[:, 0, bass.ds(g * 4 * MAPS + 4 * j, 4)]
                        dve.tensor_tensor(onehot[:, j, :, :], iota[:, :].unsqueeze(1).broadcast_to([P, 4, P]),
                                          key.unsqueeze(2).broadcast_to([P, 4, P]), ALU.is_equal)\
                            .then_inc(hot_even, 1)
                    key = chosenT[:, 1, bass.ds(g * 4 * MAPS + 4 * j, 4)]
                    dve.tensor_tensor(gatehot[:, j, :, :], iota[:, :].unsqueeze(1).broadcast_to([P, 4, P]),
                                      key.unsqueeze(2).broadcast_to([P, 4, P]), ALU.is_equal).then_inc(hot2, 1)

                def apply(g, j):
                    n = g * MAPS + (64 * (b - 1) + j)
                    dve.wait_ge(wmap, n + 1)
                    d = dense[:, :, bass.ds(g * 4 * MAPS + 4 * j, 4)].rearrange("p i t -> p t i")
                    dve.tensor_tensor(d, maps[j].rearrange("p (t i) -> p t i", t=4), d, ALU.mult)\
                        .then_inc(w_done, 1)

                for j in range(MAPS):
                    hots(0, j)
                with dve.Fori(0, 64 // MAPS - 1) as g:
                    for j in range(MAPS):
                        apply(g, j)
                        hots(g + 1, j)
                for j in range(MAPS):
                    apply(64 // MAPS - 1, j)
                r = RUNS[f"v{b}"]

                def body_v(g):
                    for j in range(GROUP):
                        u = g * GROUP + j
                        dve.wait_ge(ahi, u + (EXP_BLOCKS * (b - 1) + 1))
                        dve.tensor_tensor(act_lo[:, j % 2, :],
                                          dense[:, bass.ds(u, 1), :].rearrange("p a t -> p (a t)"),
                                          act_hi[:, j % 2, :].bitcast(F32), ALU.subtract).then_inc(alo, 1)
                        for h in range(2):
                            weight_lo(r, g, j, h)

                groups(dve, r, body_v)
                dve.wait_ge(used, r.half0 + 2 * r.units)

            def weight_lo_static(r, u, h):
                m = r.half0 + 2 * u + h
                s = m % RING
                rs = (r.unit0 + u) % RAW
                dve.wait_ge(hi_done, m + 1)
                dve.tensor_tensor(lo[:, s, :, :], raw[:, rs, 4 * h:4 * h + 4, :], hi[:, s, :, :].bitcast(F32),
                                  ALU.subtract).then_inc(lo_done, 1)

            dve.wait_ge(cols_in_s, 16)
            link(dve.tensor_scalar(neg_sinks[:, :], cols[:, COLS["sinks"][0]:COLS["sinks"][0] + 8], -1.0, None,
                                   ALU.mult))
            dve.wait_ge(ada_used, ADA_UNITS)
            link(dve.tensor_tensor(mod[:, :], bw[1][:, 0:48], cols[:, COLS["b_ada"][0]:COLS["b_ada"][0] + 48],
                                   ALU.add))
            for k, name in ((0, "norm1_g"), (1, "norm2_g")):
                at = COLS[name][0]
                link(dve.scalar_tensor_tensor(out=gain[:, k, :], in0=mod[:, 24 * k + 8:24 * k + 16], scalar=1.0,
                                              in1=cols[:, at:at + 8], op0=ALU.add, op1=ALU.mult))
            dve.engine_nop().then_inc(mod_s, 1)
            dve.wait_ge(x_in_s, 16)
            norm_apply("norm1", xT, lambda kt: gain[:, 0, kt:kt + 1], shift_k=0)
            run("ka_qa")
            for name in ("va", "qkb", "vb", "gates1"):
                run(name)
            dve.wait_ge(g_ps, 1)
            link(dve.tensor_scalar(rows[0:4, 0, :], bw[0][0:4, 0:T], col("b_i")[0:4], None, ALU.add))
            log_sigmoid(0, 4, bw[1][0:4, 0:T], col("b_f")[0:4], lambda i: rows[0:4, 1 + i, :])
            link(dve.memset(rows[0:4, 3, :], 1.0))
            link(dve.tensor_tensor_scan(rows[0:4, 4, :], rows[0:4, 3, :], rows[0:4, 1, :], 0.0, ALU.mult, ALU.add))
            link(dve.tensor_tensor(rows[0:4, 0, :], rows[0:4, 0, :], rows[0:4, 4, :], ALU.subtract))
            link(dve.tensor_tensor_scan(rows[0:4, 1, :], rows[0:4, 3, :], rows[0:4, 0, :], 0.0, ALU.mult, ALU.max))
            dve.tensor_tensor(rows[0:4, 2, :], rows[0:4, 4, :], rows[0:4, 1, :], ALU.add).then_inc(g_scan, 1)
            dve.wait_ge(taken, RUNS["gates1"].out0)
            for tap in range(4):
                for j in range(8):
                    u = upad[:, j, 1 + tap:1 + tap + T]
                    w = cols[:, COLS["conv_w"][0] + 8 * tap + j:COLS["conv_w"][0] + 8 * tap + j + 1]
                    if tap == 0:
                        ins = dve.tensor_scalar(qkc[:, j, :], u, w, col("conv_b", j), ALU.mult, ALU.add)
                    else:
                        ins = dve.scalar_tensor_tensor(out=qkc[:, j, :], in0=u, scalar=w, in1=qkc[:, j, :],
                                                       op0=ALU.mult, op1=ALU.add)
                link(ins)
            dve.engine_nop().then_inc(conv_s, 1)
            attention(0, len(ITEMS1))
            dve.wait_ge(g_tr, 1)
            dve.tensor_copy(g_col[:, :, 0:4], bw[0][:, 0:16].rearrange("p (a h) -> p a h", a=2)[:, :, 0:4])\
                .then_inc(g_col_s, 1)
            dve.wait_ge(g_col_s, 1)

            def exponents(h):
                dve.wait_ge(m_s, h + 1)
                if h >= 2:
                    dve.wait_ge(m_o, h - 1)
                for st in range(QT):
                    ins = dve.tensor_scalar(mls_w[:, h % 2, st, :], bw[h % 2][:, 0:T], g_col[:, st, h:h + 1], 0.0,
                                            ALU.subtract, ALU.max)
                ins.then_inc(m_d, 1)

            exponents(0)
            for h in range(4):
                dve.wait_ge(m_mask, h + 1)
                w = mls_w[:, h % 2, :, :].rearrange("p a t -> p (a t)")
                dve.scalar_tensor_tensor(out=w, in0=bx[h % 2], scalar=P ** -0.5, in1=w, op0=ALU.mult, op1=ALU.mult)\
                    .then_inc(m_w, 1)
                if h < 3:
                    exponents(h + 1)
                dve.wait_ge(m_o, h + 1)
                o = bx[2 + h % 2]
                d = rstd[:, 0, :]
                link(dve.tensor_scalar(d, o[:, T:2 * T], -1.0, None, ALU.mult))
                link(dve.tensor_tensor(d, d, o[:, T:2 * T], ALU.max))
                link(dve.tensor_tensor(d, d, bw[h % 2][:, T:2 * T], ALU.max))
                link(dve.reciprocal(d, d))
                ins = dve.tensor_tensor(hb[:, h, :], o[:, 0:T], d, ALU.mult)
                ins.then_inc(m_h, 1)
                dve.wait_ge(m_h, h + 1)
            dve.wait_ge(m_rstd, 1)
            for h in range(4):
                ins = dve.scalar_tensor_tensor(out=hb[:, h, :], in0=hb[:, h, :], scalar=col("mlstm_g", h),
                                               in1=tmp[:, 4 + h, :], op0=ALU.mult, op1=ALU.mult)
            link(ins)
            dve.wait_ge(taken, RUNS["branch_a"].out0)
            link(dve.tensor_tensor(ybT, hb, sig1[:, 0:4, :], ALU.mult))
            dve.wait_ge(used, RUNS["branch_a"].half0)
            split_ready(EV["branches"], (0, yaT), (4, ybT))

            def merge(sig, first, yv):
                def evict(u, p):
                    s = sig[:, bass.ds(u, 1), :].rearrange("p a t -> p (a t)")
                    d = yv[:, bass.ds(u, 1), :].rearrange("p a t -> p (a t)") if first else s
                    return dve.tensor_tensor(d, p, s, ALU.mult)
                return evict

            run("branch_a", merge(sig1[:, 4:12, :], True, y1))
            run("branch_b", merge(sig1[:, 12:20, :], False, y1))
            dve.wait_ge(taken, RUNS["wout1"].out0)
            link(dve.tensor_tensor(y1, y1, sig1[:, 12:20, :], ALU.add))
            split_ready(EV["y1"], (0, y1))

            def add_residual(gate_at):
                def evict(u, p):
                    x = xT[:, bass.ds(u, 1), :].rearrange("p a t -> p (a t)")
                    if gate_at is None:
                        return dve.tensor_tensor(x, p, x, ALU.add)
                    return dve.scalar_tensor_tensor(out=x, in0=p, scalar=mod[:, bass.ds(gate_at + u, 1)], in1=x,
                                                    op0=ALU.mult, op1=ALU.add)
                return evict

            run("wout1", add_residual(16))
            dve.wait_ge(taken, RUNS["pq1"].out0)
            dve.engine_nop().then_inc(x_ready, 1)
            norm_apply("norm2", xT, lambda kt: gain[:, 1, kt:kt + 1], shift_k=1)
            run("pq1")
            experts(1)
            for d in range(KT):
                ins = dve.scalar_tensor_tensor(out=xT[:, d, :], in0=acc[:, d, :], scalar=mod[:, 40 + d:41 + d],
                                               in1=xT[:, d, :], op0=ALU.mult, op1=ALU.add)
            ins.then_inc(x_ready, 1)
            dve.wait_ge(x_ready, 2)
            dve.wait_ge(n_rstd, NORMS.index("final") + 1)
            for kt in range(KT):
                ins = dve.scalar_tensor_tensor(out=xT[:, kt, :], in0=xT[:, kt, :], scalar=col("final_g", kt),
                                               in1=rstd[:, 1, :], op0=ALU.mult, op1=ALU.mult)
            link(ins)
            dve.engine_nop().then_inc(x_ready, 1)
            dve.wait_ge(swa_d, 1)
            for h in range(8):
                ins = dve.tensor_scalar(biasS[:, h, :, :], dist, -8.0 * 2.0 ** -(h + 1), None, ALU.mult)
            link(ins)
            dve.engine_nop().then_inc(swa_d, 1)
            norm_apply("mem", memT, lambda kt: col("mem_g", kt))
            run("mk")
            run("mv")
            dve.wait_ge(taken, RUNS["fq_fk_sq_mq"].out0)
            norm_apply("norm1_2", xT, lambda kt: col("norm1_g_2", kt))
            for name in ("fq_fk_sq_mq", "fv", "sk", "sv", "gates2"):
                run(name)
            dve.wait_ge(g_ps, 2)
            log_sigmoid(1, 8, bw[0][0:8, 0:T], col("b_forget")[0:8], lambda i: rows2[0:8, i, :])
            link(dve.memset(rows2[0:8, 3, :], 1.0))
            dve.tensor_tensor_scan(rows2[0:8, 2, :], rows2[0:8, 3, :], rows2[0:8, 0, :], 0.0, ALU.mult, ALU.add)\
                .then_inc(g_scan, 1)
            dve.wait_ge(g_tr, 2)
            dve.tensor_copy(g_col[:, :, :], bw[0][:, 0:16].rearrange("p (a h) -> p a h", a=2)).then_inc(g_col_s, 1)
            dve.wait_ge(g_col_s, 2)
            for h in range(8):
                dve.wait_ge(fox_bc, h + 1)
                for qt in range(QT):
                    ins = dve.tensor_scalar(biasF[:, h, qt, :], bw[h % 2][:, 0:T], g_col[:, qt, h:h + 1], -8.0,
                                            ALU.subtract, ALU.mult)
                ins.then_inc(dve_fox, 1)
            dve.wait_ge(dve_fox, 8)
            dve.engine_nop().then_inc(fox_d, 1)

            for i in range(len(HEAD_NORMS)):
                src, mat, d, g, n = head_norm(i)
                dve.wait_ge(hn["rstd"], i + 1)
                dve.scalar_tensor_tensor(out=src, in0=src, scalar=g, in1=hn_r[:, i % 2, 0:n], op0=ALU.mult,
                                         op1=ALU.mult).then_inc(hn["out"], 1)
            attention(len(ITEMS1), len(ITEMS))
            dve.wait_ge(att["y"], len(ITEMS))
            dve.wait_ge(used, RUNS["fox_o"].half0)
            split_ready(EV["fox_swa"], (0, oT[:, 0:8, :]))
            run("fox_o", merge(sig2[:, 0:8, :], True, y2))
            dve.wait_ge(used, RUNS["swa_o"].half0)
            split_ready(EV["mem_o"], (0, oT[:, 8:12, :]))
            run("swa_o", merge(sig2[:, 8:16, :], False, y2))
            run("mem_o", merge(sig2[:, 16:24, :], False, y2))
            dve.wait_ge(taken, RUNS["wout2"].out0)
            link(dve.tensor_tensor(y2, y2, sig2[:, 8:16, :], ALU.add))
            link(dve.tensor_tensor(y2, y2, sig2[:, 16:24, :], ALU.add))
            split_ready(EV["y2"], (0, y2))
            run("wout2", add_residual(None))
            dve.wait_ge(taken, RUNS["pq2"].out0)
            dve.engine_nop().then_inc(x_ready, 1)
            norm_apply("norm2_2", xT, lambda kt: col("norm2_g_2", kt))
            run("pq2")
            experts(2)
            for d in range(KT):
                ins = dve.tensor_tensor(xT[:, d, :], acc[:, d, :], xT[:, d, :], ALU.add)
            ins.then_inc(x_ready, 1)


def kernel(**inputs):
    import numpy as np
    import concourse.bacc as bacc
    from concourse.bass_utils import run_bass_kernel_spmd as run

    f = {k: np.asarray(v) for k, v in inputs.items()}

    def units(w):
        return w.reshape(KT, P, -1, P).transpose(2, 1, 0, 3)

    def half_units(w):
        h = w.reshape(4, P, 8, P).transpose(2, 1, 0, 3)
        return h.reshape(4, 2, P, 4, P).transpose(0, 2, 1, 3, 4).reshape(4, P, KT, P)

    def columns(v):
        return v.reshape(-1, P).T

    w_in = f["w_in"][0]
    ka, qa = w_in[:, 512:1024], w_in[:, 0:512]
    va, qkb = w_in[:, 1024:1536], w_in[:, 1536:2560]
    vb, ob = w_in[:, 2560:3072], w_in[:, 3072:3584]
    gates1 = w_in[:, 3584:3592]
    ga_gb = w_in[:, 3592:]
    front1 = np.concatenate([units(f["w_ada"][0]), units(ka), units(qa), units(va), units(qkb), units(vb), units(ob),
                             units(ga_gb), half_units(f["w_branch_a"][0]), half_units(f["w_branch_b"][0]),
                             units(f["w_out"][0]), units(f["w_peer_q"][0])])
    w2 = f["w_in_2"][0]
    fq, fk, fv, ff = w2[:, 0:512], w2[:, 512:1024], w2[:, 1024:1536], w2[:, 1536:1544]
    sq, sk, sv = w2[:, 1544:2056], w2[:, 2056:2184], w2[:, 2184:2312]
    mq, gl = w2[:, 2312:2824], w2[:, 2824:]
    sq = sq.reshape(D, 2, 4, 64).transpose(0, 2, 1, 3).reshape(D, 512)
    mkv = f["w_mem_kv_2"][0]
    front2 = np.concatenate([units(mkv[:, 0:512]), units(mkv[:, 512:]), units(fq), units(fk), units(sq), units(mq),
                             units(fv), units(sk), units(sv), units(gl), half_units(f["w_fox_o_2"][0]),
                             half_units(f["w_swa_o_2"][0]), half_units(f["w_mem_o_2"][0]), units(f["w_out_2"][0]),
                             units(f["w_peer_q_2"][0])])
    assert front1.shape[0] == FRONT[1] and front2.shape[0] == FRONT[2]

    def expert_units(u):
        return u.reshape(P, P, KT, P).transpose(1, 3, 2, 0)

    cols = np.zeros((P, N_COLS), np.float32)

    def put(name, a):
        at, n = COLS[name]
        cols[:a.shape[0], at:at + n] = a

    put("b_ada", columns(f["b_ada"][0]))
    put("norm1_g", columns(f["norm1_g"][0]))
    put("norm2_g", columns(f["norm2_g"][0]))
    put("final_g", columns(f["final_g"]))
    put("conv_b", columns(f["conv_b"][0]))
    put("conv_w", f["conv_w"][0].reshape(4, 8, P).transpose(2, 0, 1).reshape(P, 32))
    put("c", columns(f["c"][0]))
    put("mlstm_g", columns(f["mlstm_norm_g"][0]))
    put("norm1_g_2", columns(f["norm1_g_2"][0]))
    put("b_gate", columns(f["b_gate_2"][0]))
    put("mem_g", columns(f["mem_norm_g_2"][0]))
    put("norm2_g_2", columns(f["norm2_g_2"][0]))
    for name, key in (("fq_g", "fox_q_g_2"), ("fk_g", "fox_k_g_2"), ("sq_g", "swa_q_g_2"), ("sk_g", "swa_k_g_2")):
        put(name, np.tile(f[key][0], 2)[:, None])
    put("mq_g", f["mem_q_g_2"][0][:, None])
    put("mk_g", f["mem_k_g_2"][0][:, None])
    put("sinks", np.tile(f["swa_sinks_2"][0][None, :], (P, 1)))
    put("b_i", f["b_igate"][0][:, None])
    put("b_f", f["b_fgate"][0][:, None])
    put("b_forget", f["b_forget_2"][0][:, None])

    q = np.arange(T)
    rel = np.clip(q[:, None] - q[None, :], -128, 128) + 128
    biasA = f["rel_bias"][0][:, rel].reshape(8, QT, P, T).transpose(2, 0, 1, 3)
    gatew = np.stack([w.reshape(KT, P, 8).transpose(1, 0, 2) for w in (gates1, ff)])
    keys = np.stack([f["peer_sub_keys"][0].reshape(16, P, P).transpose(2, 0, 1),
                     np.stack([f["peer_keys1_2"][0], f["peer_keys2_2"][0]], axis=1).reshape(16, P, P)
                     .transpose(2, 0, 1)])
    arrays = {
        "xT_in": f["x"][0].reshape(T, KT, P).transpose(2, 1, 0),
        "memT_in": f["mem_2"][0].reshape(T, KT, P).transpose(2, 1, 0),
        "cols_in": cols, "front1": front1, "front2": front2,
        "u1": expert_units(f["peer_u"][0]), "v1": f["peer_v"][0].reshape(P, P, D),
        "u2": expert_units(f["peer_u_2"][0]), "v2": f["peer_v_2"][0].reshape(P, P, D),
        "biasA_in": biasA, "gatew_in": gatew, "keys_in": keys,
    }
    nc = bacc.Bacc("TRN2", target_bir_lowering=False, num_devices=1)
    arrays = {k: np.ascontiguousarray(a) for k, a in arrays.items()}
    args = [nc.dram_tensor(k, a.shape, F32, kind="ExternalInput").ap() for k, a in arrays.items()]
    out = nc.dram_tensor("out_T", (P, KT, T), F32, kind="ExternalOutput").ap()
    two_blocks_kernel(nc, *args, out)
    r = run(nc, [arrays], core_ids=[0])
    return r.results[0]["out_T"].transpose(2, 1, 0).reshape(1, T, D)
```

```python
from contextlib import ExitStack

import concourse.bass as bass
from concourse import mybir

F32 = mybir.dt.float32
F32R = mybir.dt.float32r
U32 = mybir.dt.uint32
ALU = mybir.AluOpType
ACT = mybir.ActivationFunctionType
AX = mybir.AxisListType

P = 128
T = 256
QT = T // P
D = 1024
KT = D // P
RAW = 4
RING = 4
GROUP = 4
EXP_BLOCKS = 128
HEADS_P = 8
TOPK = 16
N_KEYS = 128
EPS = 1e-6
NEG = -1e30
CHUNK = 64
LN_EXP = "natural_log_exp_and_others"
MAPS = 4


class Run:

    def __init__(self, name, kind, units):
        self.name, self.kind, self.units = name, kind, units


RUN_LIST = [
    Run("ka_qa", "T", 8), Run("va", "T", 4), Run("qkb", "T", 8), Run("vb", "T", 4),
    Run("gates1", "T", 20), Run("branch_a", "K", 4), Run("branch_b", "K", 4), Run("wout1", "T", 8),
    Run("pq1", "T", 16), Run("u1", "U", 128), Run("v1", "O", 128),
    Run("mk", "T", 4), Run("mv", "T", 4), Run("fq_fk_sq_mq", "T", 16), Run("fv", "T", 4),
    Run("sk", "T", 1), Run("sv", "T", 1), Run("gates2", "T", 24), Run("fox_o", "K", 4),
    Run("swa_o", "K", 4), Run("mem_o", "K", 4), Run("wout2", "T", 8), Run("pq2", "T", 16),
    Run("u2", "U", 128), Run("v2", "O", 128),
]
RUNS = {}
ADA_RING = 4
ADA_FIRST = 16
ADA_IN_RUN = {"ka_qa": (16, 2), "va": (24, 1), "qkb": (28, 2), "vb": (36, 1), "gates1": (40, 2)}


def place_runs():
    unit, half, out = 0, 0, 0
    row = {1: 0, 2: 0}
    block = 1
    for r in RUN_LIST:
        if r.name == "mk":
            block = 2
        r.unit0, r.half0, r.out0, r.block = unit, half, out, block
        if r.kind in "TK":
            r.row0 = row[block]
            row[block] += r.units
        r.outs = {"T": r.units, "K": 2 * r.units, "U": r.units, "O": 0}[r.kind]
        unit += r.units
        half += 2 * r.units
        out += r.outs
        RUNS[r.name] = r
    return row


FRONT = place_runs()

COLS = {}


def place_cols():
    at = 0
    for name, n in (("b_ada", 48), ("norm1_g", 8), ("norm2_g", 8), ("final_g", 8), ("conv_b", 8), ("conv_w", 32),
                    ("mlstm_g", 4), ("norm1_g_2", 8), ("b_gate", 24), ("mem_g", 8), ("norm2_g_2", 8),
                    ("fq_g", 1), ("fk_g", 1), ("sq_g", 1), ("sk_g", 1), ("mq_g", 1), ("mk_g", 1), ("sinks", 8),
                    ("b_i", 1), ("b_f", 1), ("b_forget", 1)):
        COLS[name] = (at, n)
        at += n
    return at


N_COLS = place_cols()

VALUES = ["va", "vb", "mv", "fv", "sv"]
EV = {n: i for i, n in enumerate(["norm1", "branches", "y1", "norm2", "mem", "norm1_2", "fox_swa", "mem_o", "y2",
                                  "norm2_2"])}
NORMS = ["norm1", "norm2", "mem", "final", "norm1_2", "norm2_2"]


def attention_items():
    return ([("a", h) for h in range(8)], [("fox", h) for h in range(8)] + [("swa", h) for h in range(8)]
            + [("mem", h) for h in range(4)])


ITEMS1, ITEMS2 = attention_items()
ITEMS = ITEMS1 + ITEMS2
HEAD_NORMS = [("mk", 0), ("mk", 2), ("mq", 0), ("mq", 2), ("fq", 0), ("fq", 2), ("fk", 0), ("fk", 2),
              ("sq", 0), ("sq", 2), ("sk", 0)]


def two_blocks_kernel(nc, xT_in, memT_in, cols_in, front1, front2, u1, v1, u2, v2, biasA_in, gatew_in, keys_in,
                      ada_in, c_in, out):
    with ExitStack() as ctx:
        def sb(name, shape, dt=F32):
            return ctx.enter_context(nc.sbuf_tensor(name, shape, dt))

        def sem(name):
            return ctx.enter_context(nc.semaphore(name))

        big = sb("big", [P, EXP_BLOCKS * T])
        raw = sb("raw", [P, RAW, KT, P])
        hi = sb("hi", [P, RING, 4, P], F32R)
        lo = sb("lo", [P, RING, 4, P], F32R)
        act_hi = sb("act_hi", [P, KT, T], F32R)
        act_lo = sb("act_lo", [P, KT, T], F32R)
        xT = sb("xT", [P, KT, T])
        scores = sb("scores", [P, QT, 16, N_KEYS])
        chosen = sb("chosen", [P, 3, QT, P])
        ident = sb("ident", [P, P])
        ones = sb("ones", [P, P])
        blockones = sb("blockones", [P, P])
        iota = sb("iota", [P, P])
        zeros = sb("zeros", [P, T])
        cols = sb("cols", [P, N_COLS])
        mod = sb("mod", [P, 48])
        gain = sb("gain", [P, 2, KT])
        small = sb("small", [P, 3, 8])
        neg_sinks = sb("neg_sinks", [P, 8])
        top = sb("top", [P, 2, TOPK])
        topi = sb("topi", [P, 2, TOPK], U32)
        ci = sb("ci", [P, TOPK], U32)
        cpart = sb("cpart", [P, 2, TOPK], U32)
        gsum = sb("gsum", [P, 16])
        eps = sb("eps", [P, 1])
        ada_sum = sb("ada_sum", [P, ADA_RING])
        g_col = sb("g_col", [P, QT, 8])

        def col(name, i=0):
            at, n = COLS[name]
            return cols[:, at + i:at + i + 1]

        def cut(at, *dims):
            n = 1
            for d in dims:
                n *= d
            v = big[:, at:at + n]
            if len(dims) == 2:
                v = v.rearrange("p (a b) -> p a b", a=dims[0])
            if len(dims) == 3:
                v = v.rearrange("p (a b c) -> p a b c", a=dims[0], b=dims[1])
            return v

        dense = big[:, :].rearrange("p (i t) -> p i t", t=T)
        biasA = cut(0, 8, QT, T)
        kaqa = cut(4096, 8, T)
        va = cut(6144, QT, 512)
        upad = cut(7168, 8, T + 4)
        vb = cut(9248, QT, 512)
        sig1 = cut(10272, 20, T)
        yaT = cut(15392, 4, T)
        qkc = cut(16416, 8, T)
        ybT = cut(18464, 4, T)
        y1 = cut(19488, 8, T)
        tmp = cut(27136, 8, T)
        att_s = cut(27136, 3, QT, T)
        att_pt = cut(30208, 2, QT, T)
        rstd = cut(31232, 2, T)
        keysA = cut(21536, 16, P)
        mls_w = cut(23584, 2, QT, T)
        vT1 = cut(23584, 4, T)
        hb = cut(24608, 4, T)
        rows = cut(25632, 5, T)
        gw = cut(26912, 2, KT, 8)
        peer_q = cut(4096, 16, T)
        ada_raw = [big[:, at:at + D] for at in (19488, 20512, 29184, 30208)]
        c_row = big[:, 31744:31744 + D]
        biasF = cut(0, 8, QT, T)
        biasS = cut(4096, 8, QT, T)
        heads16 = cut(8192, 16, T)
        skT = cut(12288, 1, T)
        mkT = cut(12544, 4, T)
        fv = cut(13568, QT, 512)
        sv = cut(14592, QT, P)
        mv = cut(14848, QT, 512)
        sig2 = cut(15872, 24, T)
        oT = cut(22016, 12, T)
        y2 = cut(25088, 8, T)
        vT2 = cut(29184, 5, T)
        dist = cut(22016, QT, T)
        hn_r = cut(25088, 4, 2 * T)
        hn_sq = cut(27136, 4, 2 * T)
        rows2 = cut(31744, 4, T)
        gw2 = cut(24576, KT, 8)
        keysB = cut(0, 16, P)
        peer_q2 = cut(2048, 16, T)

        memT = scores[:, :, :, :].rearrange("p a b c -> p (a b c)")[:, 0:KT * T].rearrange("p (a t) -> p a t", t=T)
        chosenT = chosen[:, :, :, :].rearrange("p a b c -> p a (b c)")
        flat = scores[:, :, :, :].rearrange("p a b c -> p (a b c)")
        onehot = flat[:, 0:2048].rearrange("p (b t n) -> p b t n", b=MAPS, t=4)
        gatehot = flat[:, 2048:4096].rearrange("p (b t n) -> p b t n", b=MAPS, t=4)

        ps = ctx.enter_context(nc.psum_tensor("ps", [P, 8, 512], F32))
        po = [ps[:, 0, 0:T], ps[:, 1, 0:T]]
        bx = [ps[:, 2 + i, :] for i in range(4)]
        bw = [ps[:, 6, :], ps[:, 7, :]]
        maps = [ps[:, b, :] for b in (6, 7, 0, 1)]
        bo = [ps[:, 5, 0:T], ps[:, 0, 0:T]]
        norm_at = {name: (tmp, rstd, bw[0]) for name in NORMS}
        norm_at["mem"] = (tmp, rstd, bw[1])
        norm_at["final"] = (cut(0, 8, T), cut(2048, 2, T), bw[0])
        acc = ps[:, 2:6, :].rearrange("p b (d t) -> p (b d) t", d=2)

        cols_in_s = sem("cols_loaded")
        x_in_s = sem("x_loaded")
        bias_in_s = sem("bias_loaded")
        gw_in_s = [sem("gate_weights_loaded1"), sem("gate_weights_loaded2")]
        keys_in_s = [sem("keys_loaded1"), sem("keys_loaded2")]
        mem_in_s = sem("mem_loaded")
        raw_in = [sem(f"raw_loaded{i}") for i in range(RAW)]
        consts = sem("consts_ready")
        pool_chain = sem("pool_chain")
        dve_chain = sem("dve_chain")
        act_chain = sem("act_chain")
        silu_s = sem("silu_ready")
        c_in_s = sem("c_loaded")
        ada_loaded = [sem(f"ada_loaded{i}") for i in range(ADA_RING)]
        ada_used = sem("ada_used")
        mod_s = sem("mod_ready")
        hi_done = sem("hi_done")
        lo_done = sem("lo_done")
        used = sem("halves_used")
        taken = sem("outs_taken")
        n_sq, n_sum, n_rstd = sem("norm_squares"), sem("norm_sums"), sem("norm_rstd")
        n_scaled, n_shifted = sem("norm_scaled"), sem("norm_shifted")
        act_ready = sem("activations_split")
        x_ready = sem("residual_ready")
        v_tr, v_copied = sem("values_transposed"), sem("values_copied")
        x_tile = sem("residual_tile_ready")
        att = {n: sem(f"att_{n}") for n in ("s", "m", "e", "p", "t", "c", "o", "y")}
        att_ready = sem("att_bias_ready")
        g_ps, g_row, g_exp, g_ln, g_scan, g_em = (sem(n) for n in (
            "gate_psum", "gate_rows", "gate_exp", "gate_ln", "gate_scan", "gate_em"))
        g_tr, g_col_s = sem("gate_transposed"), sem("gate_cols")
        conv_s, conv_silu = sem("conv_done"), sem("conv_silu")
        m_s, m_d, m_e, m_mask, m_w, m_o, m_h = (sem(f"mlstm_{n}") for n in (
            "scores", "exponents", "weights", "masked", "weighted", "sums", "out"))
        m_sq, m_sum, m_rstd = (sem(f"mlstm_{n}") for n in ("sq", "sum", "rstd"))
        hn = {n: sem(f"headnorm_{n}") for n in ("sq", "sum", "ln", "rstd", "out")}
        fox_bc, fox_d, swa_d = sem("fox_broadcast"), sem("fox_bias"), sem("swa_bias")
        dve_fox = sem("fox_bias_heads")
        sc_ps, sc_taken = sem("scores_psum"), sem("scores_taken")
        top_done, gate_sub, gate_exp, gate_done = (sem(n) for n in (
            "topk_done", "topgate_sub", "topgate_exp", "topgate_done"))
        ch_tr, ch_t = sem("chosen_transposed"), sem("chosen_copied")
        hot_d, hot_sq = sem("one_hot_distances"), sem("one_hot_squares")
        hot_even, hot_odd = sem("one_hots_i1_even"), sem("one_hots_i1_odd")
        hot2, hot_gate = sem("one_hots_i2"), sem("one_hots_gated")
        wmap, w_done = sem("gate_map"), sem("gate_map_applied")
        ahi, alo = sem("dense_hi"), sem("dense_lo")
        out_s = sem("out_stored")

        block = ctx.enter_context(nc.Block())

        def is_static(v):
            return isinstance(v, int)

        def groups(eng, r, body, peel=1):
            n = r.units // GROUP
            for g in range(min(peel, n)):
                body(g)
            if n > peel:
                with eng.Fori(peel, n) as g:
                    body(g)

        values = {"va": (vT1, va), "vb": (vT1, vb), "mv": (vT2[:, 0:4, :], mv), "fv": (vT2[:, 0:4, :], fv),
                  "sv": (vT2[:, 4:5, :], sv)}

        @block.sync
        def _(sp):
            def free(n):
                if is_static(n) and n < RAW:
                    return
                sp.wait_ge(lo_done, (n - RAW + 1) * 2)

            def load_ada(g, first):
                for j in range(ADA_RING):
                    if not (is_static(g) and g * ADA_RING + first < ADA_RING):
                        sp.wait_ge(ada_used, g * ADA_RING + (first + j - ADA_RING + 1))
                    sp.dma_start(ada_raw[j], ada_in[bass.ds(g * ADA_RING + (first + j), 1)]
                                 .rearrange("a p k -> (a p) k")).then_inc(ada_loaded[j], 16)

            def source(r, u):
                if r.kind == "U":
                    w = u1 if r.block == 1 else u2
                    return w[bass.ds(u, 1)].rearrange("a p k c -> (a p) k c")
                if r.kind == "O":
                    w = v1 if r.block == 1 else v2
                    return w[:, bass.ds(u, 1), :].rearrange("p a (k c) -> p (a k) c", c=P)
                w = front1 if r.block == 1 else front2
                return w[bass.ds(u + r.row0, 1)].rearrange("a p k c -> (a p) k c")

            for g in range(ADA_FIRST // ADA_RING):
                load_ada(g, 0)
            for r in RUN_LIST:
                if r.units < GROUP:
                    for u in range(r.units):
                        free(r.unit0 + u)
                        s = (r.unit0 + u) % RAW
                        sp.dma_start(raw[:, s, :, :], source(r, u)).then_inc(raw_in[s], 16)
                    continue

                def body(g, r=r):
                    for j in range(GROUP):
                        u = g * GROUP + j
                        free(u + r.unit0)
                        s = (r.unit0 + j) % RAW
                        sp.dma_start(raw[:, s, :, :], source(r, u)).then_inc(raw_in[s], 16)

                    if r.name in ADA_IN_RUN:
                        first, n = ADA_IN_RUN[r.name]
                        if is_static(g) and g < n or r.units // GROUP == n:
                            load_ada(g, first)

                groups(sp, r, body, peel=2 if r.name == "gates1" else 1)
            sp.wait_ge(x_ready, 5)
            sp.dma_start(out, xT[:, :, :]).then_inc(out_s, 16)
            sp.wait_ge(out_s, 16)

        @block.gpsimd
        def _(pool):
            n = [0]

            def link(ins):
                n[0] += 1
                ins.then_inc(pool_chain, 1)
                pool.wait_ge(pool_chain, n[0])

            def select(view, pattern, base, mult, fill, op=ALU.is_ge):
                return pool.affine_select(out=view, in_=view, compare_op=op, fill=fill, base=base, pattern=pattern,
                                          channel_multiplier=mult)

            def one_hots(b):
                pool.wait_ge(ch_t, b)

                def body(g):
                    for j in range(1, MAPS, 2):
                        n = g * (MAPS // 2) + (32 * (b - 1) + j // 2)
                        if not is_static(g):
                            pool.wait_ge(wmap, g * MAPS + (64 * (b - 1) + j - MAPS + 1))
                        key = chosenT[:, 0, bass.ds(g * 4 * MAPS + 4 * j, 4)]
                        pool.tensor_tensor(onehot[:, j, :, :], iota[:, :].unsqueeze(1).broadcast_to([P, 4, P]),
                                           key.unsqueeze(2).broadcast_to([P, 4, P]), ALU.subtract)\
                            .then_inc(hot_d, 1)
                        pool.wait_ge(hot_d, n + 1)
                        pool.tensor_tensor(onehot[:, j, :, :], onehot[:, j, :, :], onehot[:, j, :, :], ALU.mult)\
                            .then_inc(hot_sq, 1)

                body(0)
                with pool.Fori(1, 64 // MAPS) as g:
                    body(g)

            link(pool.memset(ones[:, :], 1.0))
            link(pool.memset(zeros[:, :], 0.0))
            link(pool.memset(eps[:, :], EPS))
            link(pool.memset(ident[:, :], 0.0))
            link(select(ident[:, :], [[-1, P]], 0, 1, 1.0, ALU.not_equal))
            link(pool.memset(blockones[:, :], 0.0))
            for b in range(2):
                link(pool.memset(blockones[64 * b:64 * b + 64, 64 * b:64 * b + 64], 1.0))
            link(pool.iota(iota[:, :], pattern=[[1, P]], base=0, channel_multiplier=0,
                           allow_small_or_imprecise_dtypes=True))
            link(pool.memset(upad[:, :, :], 0.0))
            pool.engine_nop().then_inc(consts, 1)
            pool.wait_ge(bias_in_s, 16)
            link(pool.tensor_scalar(biasA, biasA, 8.0, None, ALU.mult))
            for qt in range(QT):
                for half in range(2):
                    limit = CHUNK * (2 * qt + half + 1)
                    v = biasA[64 * half:64 * half + 64, :, qt, :]
                    link(select(v, [[0, 8], [-1, T]], limit - 1, 0, NEG))
            pool.engine_nop().then_inc(att_ready, 1)
            for h in range(4):
                pool.wait_ge(m_e, h + 1)
                select(mls_w[:, h % 2, :, :], [[-P, QT], [1, T]], 0, -1, 0.0).then_inc(m_mask, 1)
            one_hots(1)
            pool.wait_ge(w_done, 64)
            pool.dma_start(memT, memT_in).then_inc(mem_in_s, 16)
            pool.wait_ge(x_ready, 2)
            pool.dma_start(gw2, gatew_in[1]).then_inc(gw_in_s[1], 16)
            link(pool.iota(dist[:, :, :], pattern=[[P, QT], [-1, T]], base=0, channel_multiplier=1,
                           allow_small_or_imprecise_dtypes=True))
            pool.engine_nop().then_inc(swa_d, 1)
            pool.wait_ge(swa_d, 2)
            link(select(biasS, [[0, 8], [P, QT], [-1, T]], 0, 1, NEG))
            link(select(biasS, [[0, 8], [-P, QT], [1, T]], P - 1, -1, NEG))
            pool.wait_ge(fox_d, 1)
            link(select(biasF, [[0, 8], [P, QT], [-1, T]], 0, 1, NEG))
            pool.engine_nop().then_inc(att_ready, 1)
            pool.wait_ge(att["y"], len(ITEMS))
            pool.dma_start(keysB, keys_in[1]).then_inc(keys_in_s[1], 16)
            one_hots(2)

        def item(i):
            kind, h = ITEMS[i]
            o = 64 * (h % 2)
            if kind == "a":
                return dict(q=kaqa[o:o + 64, 4 + h // 2, :], k=kaqa[o:o + 64, h // 2, :], bias=biasA[:, h, :, :],
                            scale=64 ** -0.5, v=lambda kt: va[:, kt, 64 * h:64 * h + 64], dh=64,
                            out=yaT[o:o + 64, h // 2, :], sink=None)
            if kind == "fox":
                return dict(q=heads16[o:o + 64, h // 2, :], k=heads16[o:o + 64, 4 + h // 2, :],
                            bias=biasF[:, h, :, :], scale=64 ** -0.5, v=lambda kt: fv[:, kt, 64 * h:64 * h + 64],
                            dh=64, out=oT[o:o + 64, h // 2, :], sink=None)
            if kind == "swa":
                g = h // 4
                return dict(q=heads16[64 * g:64 * g + 64, 8 + h % 4, :], k=skT[64 * g:64 * g + 64, 0, :],
                            bias=biasS[:, h, :, :], scale=64 ** -0.5, v=lambda kt: sv[:, kt, 64 * g:64 * g + 64],
                            dh=64, out=oT[o:o + 64, 4 + h // 2, :], sink=h)
            return dict(q=heads16[:, 12 + h, :], k=mkT[:, h, :], bias=None, scale=128 ** -0.5,
                        v=lambda kt: mv[:, kt, P * h:P * h + P], dh=P, out=oT[:, 8 + h, :], sink=None)

        def head_norm(i):
            name, u = HEAD_NORMS[i]
            v = {"mk": mkT, "mq": heads16[:, 12:16, :], "fq": heads16[:, 0:4, :], "fk": heads16[:, 4:8, :],
                 "sq": heads16[:, 8:12, :], "sk": skT}[name]
            n = 1 if name == "sk" else 2
            wide = name[0] == "m"
            return v[:, u:u + n, :].rearrange("p a t -> p (a t)"), (ones if wide else blockones), \
                (128 if wide else 64), col(name + "_g"), n * T

        @block.tensor
        def _(pe):
            def norm_sum(name):
                k = NORMS.index(name)
                squares, _, sums = norm_at[name]
                for kt in range(KT):
                    pe.wait_ge(n_sq, KT * k + kt + 1)
                    mm = pe.matmul(sums[:, 0:T], ones[:, :], squares[:, kt, :], start=(kt == 0), stop=(kt == KT - 1))
                mm.then_inc(n_sum, 1)

            def three(out_ap, hi_l, lo_l, hi_r, lo_r, n, first, last, wait_lo):
                for k in range(n):
                    pe.matmul(out_ap, hi_l(k), hi_r(k), start=(first and k == 0), stop=False, skip_group_check=True)
                for k in range(n):
                    pe.matmul(out_ap, hi_l(k), lo_r(k), start=False, stop=False, skip_group_check=True)
                wait_lo()
                for k in range(n):
                    mm = pe.matmul(out_ap, lo_l(k), hi_r(k), start=False, stop=(last and k == n - 1), skip_group_check=True)
                return mm

            def half(r, g, j, h):
                m = (g * GROUP + j) * 2 + (r.half0 + h)
                s = (r.half0 + 2 * j + h) % RING
                pe.wait_ge(hi_done, m + 1)

                def wait_lo():
                    pe.wait_ge(lo_done, m + 1)

                k0 = 4 * h
                if r.kind == "K":
                    o = (r.out0 + 2 * j + h) % 2
                    c0 = 4 if r.name in ("branch_b", "swa_o") else 0
                    mm = three(po[o], lambda k: hi[:, s, k, :], lambda k: lo[:, s, k, :],
                               lambda k: act_hi[:, c0 + k, :], lambda k: act_lo[:, c0 + k, :], 4, True, True, wait_lo)
                elif r.kind in "TU":
                    o = (r.out0 + j) % 2
                    mm = three(po[o], lambda k: hi[:, s, k, :], lambda k: lo[:, s, k, :],
                               lambda k: act_hi[:, k0 + k, :], lambda k: act_lo[:, k0 + k, :], 4, h == 0, h == 1,
                               wait_lo)
                else:
                    b = j % 2
                    u = g * GROUP + j
                    base = EXP_BLOCKS * (r.block - 1)
                    if h == 0:
                        pe.wait_ge(ahi, u + (base + 1))
                        pe.wait_ge(alo, u + (base + 1))
                    for k in range(4):
                        for w, a in ((hi, act_hi), (hi, act_lo)):
                            pe.matmul(acc[:, k0 + k, :], w[:, s, k, :], a[:, b, :], start=False, stop=False,
                                      skip_group_check=True)
                    wait_lo()
                    for k in range(4):
                        mm = pe.matmul(acc[:, k0 + k, :], lo[:, s, k, :], act_hi[:, b, :], start=False, stop=False,
                                       skip_group_check=True)
                mm.then_inc(used, 1)

            def outs_free(r, o):
                if is_static(o) and o < 2:
                    return
                pe.wait_ge(taken, o - 1)

            def run(name, event=None):
                r = RUNS[name]
                if event is not None:
                    pe.wait_ge(act_ready, 2 * EV[event] + 1)
                if r.kind != "O" and r.out0:
                    pe.wait_ge(taken, r.out0)

                def body(g):
                    for j in range(min(GROUP, r.units)):
                        for h in range(2):
                            if r.kind == "K":
                                outs_free(r, (g * GROUP + j) * 2 + (r.out0 + h))
                            elif h == 0 and r.kind != "O":
                                outs_free(r, g * GROUP + (r.out0 + j))
                            if event is not None and h == 1 and is_static(g) and j == 0:
                                pe.wait_ge(act_ready, 2 * EV[event] + 2)
                            half(r, g, j, h)

                if r.units < GROUP:
                    body(0)
                else:
                    groups(pe, r, body)

            def to_tokens(name):
                k, r = VALUES.index(name), RUNS[name]
                pe.wait_ge(taken, r.out0 + r.outs)
                if k:
                    pe.wait_ge(v_copied, k)
                for tt in range(QT):
                    for u in range(r.units):
                        mm = pe.transpose(bx[tt][:, u * P:u * P + P], values[name][0][:, u, tt * P:tt * P + P],
                                          ident[:, :])
                mm.then_inc(v_tr, 1)

            def transpose(out_ap, in_ap, n):
                return pe.transpose(out_ap, in_ap, ident[0:n, 0:n])

            def attention(first, last):
                def s(i):
                    a = item(i)
                    if i >= 2:
                        pe.wait_ge(att["m"], i - 1)
                    for qt in range(QT):
                        mm = pe.matmul(bx[i % 2][:, qt * T:qt * T + T], a["q"][:, P * qt:P * qt + P], a["k"],
                                       start=True, stop=True)
                    mm.then_inc(att["s"], 1)

                def pt(i):
                    pe.wait_ge(att["p"], i + 1)
                    if i >= 1:
                        pe.wait_ge(att["c"], i)
                    for kt in range(QT):
                        for qt in range(QT):
                            mm = pe.transpose(bx[2][:, kt * T + qt * P:kt * T + qt * P + P],
                                              att_s[:, i % 3, qt, kt * P:kt * P + P], ident[:, :])
                    mm.then_inc(att["t"], 1)

                def o(i):
                    a = item(i)
                    pe.wait_ge(att["c"], i + 1)
                    if i >= 2:
                        pe.wait_ge(att["y"], i - 1)
                    for kt in range(QT):
                        mm = pe.matmul(bo[i % 2][0:a["dh"], :], a["v"](kt),
                                       att_pt[:, i % 2, kt, :], start=(kt == 0), stop=(kt == QT - 1))
                    mm.then_inc(att["o"], 1)

                s(first)
                s(first + 1)
                for i in range(first, last):
                    if i + 2 < last:
                        s(i + 2)
                    if i > first:
                        o(i - 1)
                    pt(i)
                o(last - 1)

            def broadcast_row(out_ap, rows_ap, n, h):
                return pe.matmul(out_ap, ident[0:n, h:h + 1].broadcast_to([n, P]), rows_ap, start=True, stop=True)

            def peer_scores(b, q, keys):
                pe.wait_ge(keys_in_s[b - 1], 16)
                pe.wait_ge(taken, RUNS[f"pq{b}"].out0 + 16)
                for c in range(8):
                    n = 8 * (b - 1) + c
                    if n >= 2:
                        pe.wait_ge(sc_taken, n - 1)
                    tt, p0 = c // 4, 4 * (c % 4)
                    for k in range(4):
                        mm = pe.matmul(bw[c % 2][:, k * P:k * P + P], q[:, p0 + k, tt * P:tt * P + P],
                                       keys[:, p0 + k, :], start=True, stop=True)
                    mm.then_inc(sc_ps, 1)

            def gate_map(b):
                pe.wait_ge(gate_done, b)
                for c in range(3):
                    for tt in range(QT):
                        mm = pe.transpose(bx[c][:, tt * P:tt * P + P], chosen[:, c, tt, :], ident[:, :])
                mm.then_inc(ch_tr, 1)

                def body(g):
                    for j in range(MAPS):
                        n = g * MAPS + (64 * (b - 1) + j)
                        pe.wait_ge(hot_odd if j % 2 else hot_even, g * (MAPS // 2) + (32 * (b - 1) + j // 2 + 1))
                        pe.wait_ge(hot_gate, n + 1)
                        if not is_static(n) or n >= MAPS:
                            pe.wait_ge(w_done, n - MAPS + 1)
                        for t in range(4):
                            mm = pe.matmul(maps[j][:, t * P:t * P + P], onehot[:, j, t, :], gatehot[:, j, t, :],
                                           start=True, stop=True)
                        mm.then_inc(wmap, 1)

                body(0)
                with pe.Fori(1, 64 // MAPS) as g:
                    body(g)

            def experts(b):
                peer_scores(b, peer_q if b == 1 else peer_q2, keysA if b == 1 else keysB)
                pe.wait_ge(act_ready, 2 * EV["norm2" if b == 1 else "norm2_2"] + 2)
                run(f"u{b}")
                gate_map(b)
                pe.wait_ge(ch_t, b)
                for d in range(KT):
                    pe.matmul(acc[:, d, :], zeros[:, 0:P], zeros[:, :], start=(d % 2 == 0), stop=False,
                              skip_group_check=True)
                run(f"v{b}")

            pe.wait_ge(consts, 1)
            norm_sum("norm1")
            run("ka_qa", "norm1")
            pe.wait_ge(act_ready, 2 * EV["norm1"] + 2)
            pe.wait_ge(gw_in_s[0], 16)
            for c in range(2):
                for kt in range(KT):
                    mm = pe.matmul(bw[c][0:4, 0:T], gw[:, 0, kt, 4 * c:4 * c + 4], tmp[:, kt, :],
                                   start=(kt == 0), stop=(kt == KT - 1))
            mm.then_inc(g_ps, 1)
            run("va")
            run("qkb")
            to_tokens("va")
            run("vb")
            run("gates1")
            to_tokens("vb")
            pe.wait_ge(v_copied, 2)
            pe.wait_ge(taken, RUNS["gates1"].out0 + 20)
            pe.wait_ge(att_ready, 1)
            attention(0, len(ITEMS1))
            pe.wait_ge(act_ready, 2 * EV["branches"] + 1)
            run("branch_a")
            pe.wait_ge(g_scan, 1)
            for tt in range(QT):
                mm = transpose(bw[0][:, 8 * tt:8 * tt + 4], rows[0:4, 0, tt * P:tt * P + P], 4)
            mm.then_inc(g_tr, 1)
            pe.wait_ge(g_em, 1)
            pe.wait_ge(g_col_s, 1)
            pe.wait_ge(conv_silu, 1)
            pe.wait_ge(att["y"], len(ITEMS1))

            def mlstm_scores(h):
                if h >= 2:
                    pe.wait_ge(m_w, h - 1)
                    pe.wait_ge(m_h, h - 1)
                for st in range(QT):
                    pe.matmul(bx[h % 2][:, st * T:st * T + T], qkc[:, 4 + h, st * P:st * P + P], qkc[:, h, :],
                              start=True, stop=True)
                broadcast_row(bw[h % 2][:, 0:T], rows[0:4, 1, :], 4, h)
                broadcast_row(bw[h % 2][:, T:2 * T], rows[0:4, 2, :], 4, h).then_inc(m_s, 1)

            def mlstm_sums(h):
                pe.wait_ge(m_w, h + 1)
                o = bx[2 + h % 2]
                for st in range(QT):
                    pe.matmul(o[:, 0:T], vb[:, st, h * P:h * P + P], mls_w[:, h % 2, st, :], start=(st == 0),
                              stop=(st == 1))
                for st in range(QT):
                    mm = pe.matmul(o[:, T:2 * T], ones[:, :], mls_w[:, h % 2, st, :], start=(st == 0),
                                   stop=(st == 1))
                mm.then_inc(m_o, 1)

            for h in (0, 2):
                mlstm_scores(h)
                mlstm_scores(h + 1)
                mlstm_sums(h)
                mlstm_sums(h + 1)
            pe.wait_ge(m_sq, 1)
            for h in range(4):
                mm = pe.matmul(bx[h // 2][:, (h % 2) * T:(h % 2) * T + T], ones[:, :], tmp[:, h, :], start=True,
                               stop=True)
            mm.then_inc(m_sum, 1)
            pe.wait_ge(act_ready, 2 * EV["branches"] + 2)
            run("branch_b")
            run("wout1", "y1")
            norm_sum("norm2")
            run("pq1", "norm2")
            experts(1)
            norm_sum("mem")
            norm_sum("final")
            run("mk", "mem")
            run("mv")
            to_tokens("mv")
            norm_sum("norm1_2")
            pe.wait_ge(act_ready, 2 * EV["norm1_2"] + 2)
            pe.wait_ge(gw_in_s[1], 16)
            for kt in range(KT):
                mm = pe.matmul(bw[0][0:8, 0:T], gw2[:, kt, :], tmp[:, kt, :], start=(kt == 0), stop=(kt == KT - 1))
            mm.then_inc(g_ps, 1)
            run("fq_fk_sq_mq")
            run("fv")
            run("sk")
            run("sv")
            run("gates2")
            to_tokens("fv")
            to_tokens("sv")
            pe.wait_ge(v_copied, len(VALUES))
            pe.wait_ge(g_scan, 2)
            for tt in range(QT):
                mm = transpose(bw[0][:, 8 * tt:8 * tt + 8], rows2[0:8, 2, tt * P:tt * P + P], 8)
            mm.then_inc(g_tr, 1)
            pe.wait_ge(g_col_s, 2)
            for h in range(8):
                if h >= 2:
                    pe.wait_ge(dve_fox, h - 1)
                broadcast_row(bw[h % 2][:, 0:T], rows2[0:8, 2, :], 8, h).then_inc(fox_bc, 1)
            for i in range(len(HEAD_NORMS)):
                src, mat, d, g, n = head_norm(i)
                pe.wait_ge(hn["sq"], i + 1)
                if i >= 4:
                    pe.wait_ge(hn["ln"], i - 3)
                pe.matmul(bx[i % 4][:, 0:n], mat[:, :], hn_sq[:, i % 4, 0:n], start=True, stop=True)\
                    .then_inc(hn["sum"], 1)
            pe.wait_ge(hn["out"], len(HEAD_NORMS))
            pe.wait_ge(att_ready, 2)
            attention(len(ITEMS1), len(ITEMS))
            pe.wait_ge(act_ready, 2 * EV["fox_swa"] + 2)
            run("fox_o")
            run("swa_o")
            pe.wait_ge(act_ready, 2 * EV["mem_o"] + 2)
            run("mem_o")
            run("wout2", "y2")
            norm_sum("norm2_2")
            run("pq2", "norm2_2")
            experts(2)

        @block.scalar
        def _(act):
            n_chain = [0]

            def link(ins):
                n_chain[0] += 1
                ins.then_inc(act_chain, 1)
                act.wait_ge(act_chain, n_chain[0])

            act.dma_start(c_row, c_in.broadcast_to([P, D])).then_inc(c_in_s, 16)
            act.dma_start(cols[:, :], cols_in).then_inc(cols_in_s, 16)
            act.dma_start(xT[:, :, :], xT_in).then_inc(x_in_s, 16)
            act.dma_start(gw, gatew_in.rearrange("b p k c -> p b k c")).then_inc(gw_in_s[0], 16)

            def weight_hi(r, g, j, h):
                m = (g * GROUP + j) * 2 + (r.half0 + h)
                s = (r.half0 + 2 * j + h) % RING
                rs = (r.unit0 + j) % RAW
                if h == 0:
                    act.wait_ge(raw_in[rs], g * 16 + 16 * ((r.unit0 + j) // RAW + 1))
                if not (is_static(m) and m < RING):
                    act.wait_ge(used, m - RING + 1)
                act.activation(hi[:, s, :, :], raw[:, rs, 4 * h:4 * h + 4, :], ACT.Copy).then_inc(hi_done, 1)

            def run(name, evict=None):
                r = RUNS[name]

                def body(g):
                    for j in range(min(GROUP, r.units)):
                        for h in range(2):
                            weight_hi(r, g, j, h)
                        if evict and not (j == 0 and is_static(g) and g == 0):
                            out(g * GROUP + (j - 1), (r.out0 + j - 1) % 2)

                def out(u, b):
                    act.wait_ge(used, u * 2 + (r.half0 + 2))
                    evict(u, po[b]).then_inc(taken, 1)

                if r.units < GROUP:
                    body(0)
                else:
                    groups(act, r, body)
                if evict:
                    out(r.units - 1, (r.out0 + r.units - 1) % 2)

            def to(dst, func=ACT.Copy):
                return lambda u, p: act.activation(dst[:, bass.ds(u, 1), :].rearrange("p a t -> p (a t)"), p, func)

            def copy_tokens(name):
                k, r = VALUES.index(name), RUNS[name]
                act.wait_ge(v_tr, k + 1)
                for tt in range(QT):
                    ins = act.activation(values[name][1][:, tt, :], bx[tt][:, 0:r.units * P], ACT.Copy)
                ins.then_inc(v_copied, 1)

            def norm_squares(name, src, tile_ready=None):
                act.preload_act_table_set(LN_EXP)
                for kt in range(KT):
                    if tile_ready is not None:
                        act.wait_ge(tile_ready[0], tile_ready[1] + kt + 1)
                    act.activation(norm_at[name][0][:, kt, :], src[:, kt, :], ACT.Square).then_inc(n_sq, 1)

            def norm_rstd(name):
                act.wait_ge(n_sum, NORMS.index(name) + 1)
                _, r, sums = norm_at[name]
                link(act.activation(r[:, 0, :], sums[:, 0:T], ACT.Ln, bias=eps[:, :], scale=1.0 / D))
                act.activation(r[:, 1, :], r[:, 0, :], ACT.Exp, scale=-0.5).then_inc(n_rstd, 1)

            def norm_shift(k, at):
                for kt in range(KT):
                    act.wait_ge(n_scaled, 8 * k + kt + 1)
                    act.activation(tmp[:, kt, :], tmp[:, kt, :], ACT.Identity, bias=mod[:, at + kt:at + kt + 1])\
                        .then_inc(n_shifted, 1)

            def attention(first, last):
                def exps(i):
                    a = item(i)
                    act.wait_ge(att["m"], i + 1)
                    sm = small[:, i % 3, :]
                    if a["sink"] is not None:
                        for qt in range(QT):
                            act.activation(sm[:, 4 + qt:5 + qt], col("sinks", a["sink"]), ACT.Exp,
                                           bias=sm[:, qt:qt + 1])
                    for qt in range(QT):
                        ins = act.activation(att_s[:, i % 3, qt, :], att_s[:, i % 3, qt, :], ACT.Exp,
                                             bias=sm[:, qt:qt + 1], scale=-1.0, accum_out=sm[:, 2 + qt:3 + qt])
                    ins.then_inc(att["e"], 1)

                def copy(i):
                    act.wait_ge(att["t"], i + 1)
                    if i >= 2:
                        act.wait_ge(att["o"], i - 1)
                    act.activation(att_pt[:, i % 2, :, :].rearrange("p a t -> p (a t)"), bx[2], ACT.Copy)\
                        .then_inc(att["c"], 1)

                exps(first)
                exps(first + 1)
                for i in range(first, last):
                    if i + 2 < last:
                        exps(i + 2)
                    copy(i)

            def log_gate(k, r):
                act.wait_ge(g_row, k + 1)
                act.activation(r, r, ACT.Exp, scale=-1.0).then_inc(g_exp, 1)
                act.wait_ge(g_exp, k + 1)
                act.activation(r, r, ACT.Ln, bias=ones[0:r.shape[0], 0:1]).then_inc(g_ln, 1)

            def experts(b):
                for c in range(8):
                    act.wait_ge(sc_ps, 8 * (b - 1) + c + 1)
                    act.activation(scores[:, c // 4, 4 * (c % 4):4 * (c % 4) + 4, :].rearrange("p a n -> p (a n)"),
                                   bw[c % 2], ACT.Copy).then_inc(sc_taken, 1)
                act.preload_act_table(ACT.Gelu_apprx_tanh if b == 1 else ACT.Gelu)
                run(f"u{b}", to(dense, ACT.Gelu_apprx_tanh if b == 1 else ACT.Gelu))
                act.wait_ge(gate_sub, b)
                g = chosen[:, 2, :, :].rearrange("p a b -> p (a b)")
                act.activation(g, g, ACT.Exp).then_inc(gate_exp, 1)
                act.wait_ge(ch_t, b)

                def gate_hots(g):
                    for j in range(MAPS):
                        if j % 2:
                            act.wait_ge(hot_sq, g * (MAPS // 2) + (32 * (b - 1) + j // 2 + 1))
                            act.activation(onehot[:, j, :, :], onehot[:, j, :, :], ACT.Relu, bias=ones[:, 0:1],
                                           scale=-1.0).then_inc(hot_odd, 1)
                        act.wait_ge(hot2, g * MAPS + (64 * (b - 1) + j + 1))
                        for t in range(4):
                            tok = g * 4 * MAPS + (4 * j + t)
                            ins = act.activation(gatehot[:, j, t, :], gatehot[:, j, t, :], ACT.Copy,
                                                 scale=chosenT[:, 2, bass.ds(tok, 1)])
                        ins.then_inc(hot_gate, 1)

                gate_hots(0)
                with act.Fori(1, 64 // MAPS) as g:
                    gate_hots(g)
                r = RUNS[f"v{b}"]
                act.wait_ge(w_done, 64 * b)

                def body(g):
                    for j in range(GROUP):
                        u = g * GROUP + j
                        base = EXP_BLOCKS * (b - 1)
                        if is_static(g) and g == 0 and j < 2:
                            act.wait_ge(used, r.half0)
                        else:
                            act.wait_ge(used, u * 2 + (r.half0 - 2))
                        act.activation(act_hi[:, j % 2, :], dense[:, bass.ds(u, 1), :].rearrange("p a t -> p (a t)"),
                                       ACT.Copy).then_inc(ahi, 1)
                        for h in range(2):
                            weight_hi(r, g, j, h)

                groups(act, r, body)

            act.wait_ge(c_in_s, 16)
            act.activation(c_row, c_row, ACT.Silu).then_inc(silu_s, 1)
            act.wait_ge(x_in_s, 16)
            act.wait_ge(consts, 1)
            norm_squares("norm1", xT)
            norm_rstd("norm1")
            norm_shift(0, 0)
            act.dma_start(biasA, biasA_in).then_inc(bias_in_s, 16)
            act.dma_start(keysA, keys_in[0]).then_inc(keys_in_s[0], 16)
            act.preload_act_table(ACT.Copy)
            run("ka_qa", to(kaqa))
            run("va", to(vT1))
            run("qkb", lambda u, p: act.activation(
                upad[:, bass.ds(u, 1), 4:4 + T].rearrange("p a t -> p (a t)"), p, ACT.Copy))
            copy_tokens("va")
            run("vb", to(vT1))
            act.preload_act_table(ACT.Sigmoid)
            run("gates1", to(sig1, ACT.Sigmoid))
            copy_tokens("vb")
            log_gate(0, rows[0:4, 2, :])
            act.wait_ge(g_scan, 1)
            act.activation(rows[0:4, 2, :], rows[0:4, 2, :], ACT.Exp, scale=-1.0).then_inc(g_em, 1)
            act.wait_ge(conv_s, 4)
            act.activation(qkc, qkc, ACT.Silu).then_inc(conv_silu, 1)
            attention(0, len(ITEMS1))
            run("branch_a")
            for h in range(4):
                act.wait_ge(m_d, h + 1)
                w = mls_w[:, h % 2, :, :]
                act.activation(w, w, ACT.Exp, scale=-1.0).then_inc(m_e, 1)
            act.wait_ge(m_h, 4)
            act.activation(tmp[:, 0:4, :], hb, ACT.Square).then_inc(m_sq, 1)
            act.preload_act_table_set(LN_EXP)
            act.wait_ge(m_sum, 1)
            for c in range(2):
                ins = act.activation(tmp[:, 2 * c:2 * c + 2, :].rearrange("p a t -> p (a t)"), bx[c], ACT.Ln,
                                     bias=eps[:, :], scale=1.0 / P)
            link(ins)
            act.activation(tmp[:, 4:8, :], tmp[:, 0:4, :], ACT.Exp, scale=-0.5).then_inc(m_rstd, 1)
            run("branch_b")
            run("wout1")
            norm_squares("norm2", xT, (taken, RUNS["wout1"].out0))
            norm_rstd("norm2")
            norm_shift(1, 24)
            run("pq1", to(peer_q))
            experts(1)
            act.wait_ge(mem_in_s, 16)
            norm_squares("mem", memT)
            norm_squares("final", xT, (x_tile, 0))
            norm_rstd("mem")
            norm_rstd("final")
            run("mk", to(mkT))
            run("mv", to(values["mv"][0]))
            copy_tokens("mv")
            act.wait_ge(x_ready, 3)
            act.wait_ge(act_ready, 2 * EV["mem"] + 2)
            norm_squares("norm1_2", xT)
            norm_rstd("norm1_2")
            act.preload_act_table(ACT.Copy)
            run("fq_fk_sq_mq", to(heads16))
            run("fv", to(values["fv"][0]))
            run("sk", to(skT))
            run("sv", to(values["sv"][0]))
            act.preload_act_table(ACT.Sigmoid)
            run("gates2", lambda u, p: act.activation(
                sig2[:, bass.ds(u, 1), :].rearrange("p a t -> p (a t)"), p, ACT.Sigmoid,
                bias=cols[:, bass.ds(COLS["b_gate"][0] + u, 1)]))
            copy_tokens("fv")
            copy_tokens("sv")
            log_gate(1, rows2[0:8, 1, :])

            def hn_squares(batch):
                for i in batch:
                    src, mat, d, g, n = head_norm(i)
                    if i >= 4:
                        act.wait_ge(hn["sum"], i - 3)
                    act.activation(hn_sq[:, i % 4, 0:n], src, ACT.Square).then_inc(hn["sq"], 1)

            act.preload_act_table_set(LN_EXP)
            act.wait_ge(taken, RUNS["gates2"].out0 + 24)
            batches = [range(i, min(i + 4, len(HEAD_NORMS))) for i in range(0, len(HEAD_NORMS), 4)]
            hn_squares(batches[0])
            for k, batch in enumerate(batches):
                for i in batch:
                    src, mat, d, g, n = head_norm(i)
                    act.wait_ge(hn["sum"], i + 1)
                    if i >= 4:
                        act.wait_ge(hn["out"], i - 3)
                    act.activation(hn_r[:, i % 4, 0:n], bx[i % 4][:, 0:n], ACT.Ln, bias=eps[:, :], scale=1.0 / d)\
                        .then_inc(hn["ln"], 1)
                if k + 1 < len(batches):
                    hn_squares(batches[k + 1])
                for i in batch:
                    n = head_norm(i)[4]
                    act.wait_ge(hn["ln"], i + 1)
                    act.activation(hn_r[:, i % 4, 0:n], hn_r[:, i % 4, 0:n], ACT.Exp, scale=-0.5)\
                        .then_inc(hn["rstd"], 1)
            attention(len(ITEMS1), len(ITEMS))
            for name in ("fox_o", "swa_o", "mem_o", "wout2"):
                run(name)
            norm_squares("norm2_2", xT, (taken, RUNS["wout2"].out0))
            norm_rstd("norm2_2")
            run("pq2", to(peer_q2))
            experts(2)

        @block.vector
        def _(dve):
            n_chain = [0]

            def link(ins):
                n_chain[0] += 1
                ins.then_inc(dve_chain, 1)
                dve.wait_ge(dve_chain, n_chain[0])

            def weight_lo(r, g, j, h):
                m = (g * GROUP + j) * 2 + (r.half0 + h)
                s = (r.half0 + 2 * j + h) % RING
                rs = (r.unit0 + j) % RAW
                dve.wait_ge(hi_done, m + 1)
                dve.tensor_tensor(lo[:, s, :, :], raw[:, rs, 4 * h:4 * h + 4, :], hi[:, s, :, :].bitcast(F32),
                                  ALU.subtract).then_inc(lo_done, 1)

            def convolution(tap):
                if tap == 0:
                    dve.wait_ge(taken, RUNS["qkb"].out0 + RUNS["qkb"].outs)
                for j in range(8):
                    u = upad[:, j, 1 + tap:1 + tap + T]
                    w = cols[:, COLS["conv_w"][0] + 8 * tap + j:COLS["conv_w"][0] + 8 * tap + j + 1]
                    if tap == 0:
                        ins = dve.tensor_scalar(qkc[:, j, :], u, w, col("conv_b", j), ALU.mult, ALU.add)
                    else:
                        ins = dve.scalar_tensor_tensor(out=qkc[:, j, :], in0=u, scalar=w, in1=qkc[:, j, :],
                                                       op0=ALU.mult, op1=ALU.add)
                    if j == 7:
                        ins.then_inc(conv_s, 1)
                        dve.wait_ge(conv_s, tap + 1)

            def ada(g, first):
                for j in range(ADA_RING):
                    dve.wait_ge(ada_loaded[j], g * 16 + 16 * (first // ADA_RING + 1))
                    dve.tensor_tensor_reduce(out=ada_raw[j], in0=ada_raw[j], in1=c_row, scale=1.0, scalar=0.0,
                                             op0=ALU.mult, op1=ALU.add, accum_out=ada_sum[:, j:j + 1])\
                        .then_inc(ada_used, 1)
                dve.wait_ge(ada_used, g * ADA_RING + (first + ADA_RING))
                ins = dve.tensor_tensor(mod[:, bass.ds(g * ADA_RING + first, ADA_RING)], ada_sum[:, :],
                                        cols[:, bass.ds(g * ADA_RING + (first + COLS["b_ada"][0]), ADA_RING)],
                                        ALU.add)
                ins.then_inc(mod_s, 1)
                dve.wait_ge(mod_s, g + (first // ADA_RING + 1))

            def run(name, evict=None):
                r = RUNS[name]
                per = 2 if r.kind == "K" else 1

                def out(u, b):
                    dve.wait_ge(used, (u * 2 // per) + (r.half0 + 2 // per) if is_static(u) else
                                u * (2 // per) + (r.half0 + 2 // per))
                    evict(u, po[b]).then_inc(taken, 1)

                def body(g):
                    for j in range(min(GROUP, r.units)):
                        for h in range(2):
                            weight_lo(r, g, j, h)
                            if evict and per == 2 and not (is_static(g) and g == 0 and j == 0 and h == 0):
                                out(g * GROUP * 2 + (2 * j + h - 1), (r.out0 + 2 * j + h - 1) % 2)
                        if evict and per == 1 and not (is_static(g) and g == 0 and j == 0):
                            out(g * GROUP + (j - 1), (r.out0 + j - 1) % 2)
                    if name in ADA_IN_RUN:
                        first, n = ADA_IN_RUN[name]
                        if is_static(g) and g < n or r.units // GROUP == n:
                            ada(g, first)
                    if name == "gates1" and g >= 1:
                        convolution(g - 1)

                if r.units < GROUP:
                    body(0)
                else:
                    groups(dve, r, body, peel=5 if name == "gates1" else 1)
                if evict:
                    out(r.outs - 1, (r.out0 + r.outs - 1) % 2)

            def split_ready(event, *parts):
                if len(parts) == 1 and parts[0][1].shape[1] > 1:
                    n = parts[0][1].shape[1] // 2
                    parts = (0, parts[0][1][:, 0:n, :]), (n, parts[0][1][:, n:2 * n, :])
                for c, src in parts:
                    split_part(c, src)

            def split_part(c, src):
                n = src.shape[1]
                link(dve.tensor_copy(act_hi[:, c:c + n, :], src))
                dve.tensor_tensor(act_lo[:, c:c + n, :], src, act_hi[:, c:c + n, :].bitcast(F32),
                                  ALU.subtract).then_inc(act_ready, 1)

            def norm_apply(name, src, gains, shift_k=None):
                dve.wait_ge(n_rstd, NORMS.index(name) + 1)
                for kt in range(KT):
                    dve.scalar_tensor_tensor(out=tmp[:, kt, :], in0=src[:, kt, :], scalar=gains(kt),
                                             in1=rstd[:, 1, :], op0=ALU.mult, op1=ALU.mult).then_inc(n_scaled, 1)
                dve.wait_ge(n_scaled, n_scaled_at[name])
                for c in (0, 4):
                    if shift_k is not None:
                        dve.wait_ge(n_shifted, 8 * shift_k + c + 4)
                    split_part(c, tmp[:, c:c + 4, :])

            n_scaled_at = {"norm1": 8, "norm2": 16, "mem": 24, "norm1_2": 32, "norm2_2": 40}

            def attention(first, last):
                def bias_max(i):
                    a = item(i)
                    dve.wait_ge(att["s"], i + 1)
                    if i >= 3:
                        dve.wait_ge(att["t"], i - 2)
                    for qt in range(QT):
                        bias = zeros[:, :] if a["bias"] is None else a["bias"][:, qt, :]
                        start = 3e38 if a["sink"] is None else neg_sinks[:, a["sink"]:a["sink"] + 1]
                        ins = dve.tensor_tensor_reduce(out=att_s[:, i % 3, qt, :], in0=bx[i % 2][:, qt * T:qt * T + T],
                                                       in1=bias, scale=-a["scale"], scalar=start, op0=ALU.add,
                                                       op1=ALU.min, accum_out=small[:, i % 3, qt:qt + 1])
                    ins.then_inc(att["m"], 1)

                def normalise(i):
                    a = item(i)
                    dve.wait_ge(att["e"], i + 1)
                    sm = small[:, i % 3, :]
                    if a["sink"] is not None:
                        link(dve.tensor_tensor(sm[:, 2:4], sm[:, 2:4], sm[:, 4:6], ALU.add))
                    link(dve.reciprocal(sm[:, 6:8], sm[:, 2:4]))
                    for qt in range(QT):
                        ins = dve.tensor_scalar(att_s[:, i % 3, qt, :], att_s[:, i % 3, qt, :], sm[:, 6 + qt:7 + qt],
                                                None, ALU.mult)
                    ins.then_inc(att["p"], 1)

                def take(i):
                    a = item(i)
                    dve.wait_ge(att["o"], i + 1)
                    dve.tensor_copy(a["out"], bo[i % 2][0:a["dh"], :]).then_inc(att["y"], 1)

                bias_max(first)
                bias_max(first + 1)
                for i in range(first, last):
                    normalise(i)
                    if i + 2 < last:
                        bias_max(i + 2)
                    if i > first:
                        take(i - 1)
                take(last - 1)

            def log_sigmoid(k, n, f_ps, bias, r):
                link(dve.tensor_scalar(r(0), f_ps, bias, None, ALU.add))
                link(dve.scalar_tensor_tensor(out=r(1), in0=r(0), scalar=-1.0, in1=r(0), op0=ALU.mult, op1=ALU.max))
                dve.tensor_scalar(r(0), r(0), 0.0, None, ALU.min).then_inc(g_row, 1)
                dve.wait_ge(g_ln, k + 1)
                link(dve.tensor_tensor(r(0), r(0), r(1), ALU.subtract))

            def topk_scores(tt, pair):
                s = scores[:, tt, pair, :]
                p = pair % 2
                for half in range(2):
                    c = slice(8 * half, 8 * half + 8)
                    link(dve.max(top[:, p, c], s))
                    link(dve.max_index(topi[:, p, c], top[:, p, c], s))
                    if half == 0:
                        link(dve.match_replace(s, top[:, p, c], s, -3e38))

            cand = bw[0][:, 0:T].rearrange("p (a b) -> p a b", a=TOPK)
            same = bw[1][:, 0:T].rearrange("p (a b) -> p a b", a=TOPK)

            def topk_pairs(tt, h):
                link(dve.tensor_tensor(cand, top[:, 0, :].unsqueeze(2).broadcast_to([P, TOPK, TOPK]),
                                       top[:, 1, :].unsqueeze(1).broadcast_to([P, TOPK, TOPK]), ALU.add))
                flat_c = bw[0][:, 0:T]
                best = chosen[:, 2, tt, TOPK * h:TOPK * h + TOPK]
                for half in range(2):
                    c = slice(8 * half, 8 * half + 8)
                    link(dve.max(best[:, c], flat_c))
                    link(dve.max_index(ci[:, c], best[:, c], flat_c))
                    if half == 0:
                        link(dve.match_replace(flat_c, best[:, c], flat_c, -3e38))

            def topk_experts(tt, h):
                link(dve.tensor_scalar(cpart[:, 0, :], ci[:, :], 4, None, ALU.logical_shift_right))
                link(dve.tensor_scalar(cpart[:, 1, :], ci[:, :], 15, None, ALU.bitwise_and))
                for p in range(2):
                    rank = cpart[:, p, :].unsqueeze(2).broadcast_to([P, TOPK, TOPK])
                    key = topi[:, p, :].unsqueeze(1).broadcast_to([P, TOPK, TOPK])
                    link(dve.tensor_tensor(same, rank, iota[:, 0:TOPK].unsqueeze(1).broadcast_to([P, TOPK, TOPK]),
                                           ALU.is_equal))
                    link(dve.tensor_tensor(same, same, key, ALU.mult))
                    link(dve.tensor_reduce(chosen[:, p, tt, TOPK * h:TOPK * h + TOPK], same, AX.X, ALU.add))

            def experts(b):
                r = RUNS[f"u{b}"]
                dve.wait_ge(sc_taken, 8 * b)
                step = 0
                for u in range(r.units):
                    for h in range(2):
                        weight_lo_static(r, u, h)
                    if u >= 4 and u % 7 in (0, 1, 3, 5) and step < 64:
                        tt, rest = step // 32, step % 32
                        head, part = rest // 4, rest % 4
                        if part < 2:
                            topk_scores(tt, 2 * head + part)
                        elif part == 2:
                            topk_pairs(tt, head)
                        else:
                            topk_experts(tt, head)
                        step += 1
                assert step == 64
                g = chosen[:, 2, :, :].rearrange("p a (h k) -> p (a h) k", k=TOPK)
                link(dve.tensor_copy(gsum[:, :], g[:, :, 0:1].rearrange("p a k -> p (a k)")))
                dve.tensor_tensor(g, g, gsum[:, :].unsqueeze(2).broadcast_to([P, 16, TOPK]), ALU.subtract)\
                    .then_inc(gate_sub, 1)
                dve.wait_ge(gate_exp, b)
                link(dve.tensor_reduce(gsum[:, :], g, AX.X, ALU.add))
                link(dve.reciprocal(gsum[:, :], gsum[:, :]))
                dve.tensor_tensor(g, g, gsum[:, :].unsqueeze(2).broadcast_to([P, 16, TOPK]), ALU.mult)\
                    .then_inc(gate_done, 1)
                dve.wait_ge(ch_tr, b)
                for c in range(3):
                    ins = dve.tensor_copy(chosenT[:, c, :], bx[c][:, 0:T])
                link(ins)
                dve.engine_nop().then_inc(ch_t, 1)
                dve.wait_ge(taken, r.out0 + r.outs)

                def hots(g, j):
                    if j % 2 == 0:
                        key = chosenT[:, 0, bass.ds(g * 4 * MAPS + 4 * j, 4)]
                        dve.tensor_tensor(onehot[:, j, :, :], iota[:, :].unsqueeze(1).broadcast_to([P, 4, P]),
                                          key.unsqueeze(2).broadcast_to([P, 4, P]), ALU.is_equal)\
                            .then_inc(hot_even, 1)
                    key = chosenT[:, 1, bass.ds(g * 4 * MAPS + 4 * j, 4)]
                    dve.tensor_tensor(gatehot[:, j, :, :], iota[:, :].unsqueeze(1).broadcast_to([P, 4, P]),
                                      key.unsqueeze(2).broadcast_to([P, 4, P]), ALU.is_equal).then_inc(hot2, 1)

                def apply(g, j):
                    n = g * MAPS + (64 * (b - 1) + j)
                    dve.wait_ge(wmap, n + 1)
                    d = dense[:, :, bass.ds(g * 4 * MAPS + 4 * j, 4)].rearrange("p i t -> p t i")
                    dve.tensor_tensor(d, maps[j].rearrange("p (t i) -> p t i", t=4), d, ALU.mult)\
                        .then_inc(w_done, 1)

                for j in range(MAPS):
                    hots(0, j)
                with dve.Fori(0, 64 // MAPS - 1) as g:
                    for j in range(MAPS):
                        apply(g, j)
                        hots(g + 1, j)
                for j in range(MAPS):
                    apply(64 // MAPS - 1, j)
                r = RUNS[f"v{b}"]

                def body_v(g):
                    for j in range(GROUP):
                        u = g * GROUP + j
                        dve.wait_ge(ahi, u + (EXP_BLOCKS * (b - 1) + 1))
                        dve.tensor_tensor(act_lo[:, j % 2, :],
                                          dense[:, bass.ds(u, 1), :].rearrange("p a t -> p (a t)"),
                                          act_hi[:, j % 2, :].bitcast(F32), ALU.subtract).then_inc(alo, 1)
                        for h in range(2):
                            weight_lo(r, g, j, h)

                groups(dve, r, body_v)
                dve.wait_ge(used, r.half0 + 2 * r.units)

            def weight_lo_static(r, u, h):
                m = r.half0 + 2 * u + h
                s = m % RING
                rs = (r.unit0 + u) % RAW
                dve.wait_ge(hi_done, m + 1)
                dve.tensor_tensor(lo[:, s, :, :], raw[:, rs, 4 * h:4 * h + 4, :], hi[:, s, :, :].bitcast(F32),
                                  ALU.subtract).then_inc(lo_done, 1)

            dve.wait_ge(cols_in_s, 16)
            link(dve.tensor_scalar(neg_sinks[:, :], cols[:, COLS["sinks"][0]:COLS["sinks"][0] + 8], -1.0, None,
                                   ALU.mult))
            dve.wait_ge(silu_s, 1)
            for g in range(ADA_FIRST // ADA_RING):
                ada(g, 0)

            def gains(k, name):
                at = COLS[name][0]
                link(dve.scalar_tensor_tensor(out=gain[:, k, :], in0=mod[:, 24 * k + 8:24 * k + 16], scalar=1.0,
                                              in1=cols[:, at:at + 8], op0=ALU.add, op1=ALU.mult))

            gains(0, "norm1_g")
            dve.wait_ge(x_in_s, 16)
            norm_apply("norm1", xT, lambda kt: gain[:, 0, kt:kt + 1], shift_k=0)
            for name in ("ka_qa", "va", "qkb", "vb", "gates1"):
                run(name)
            gains(1, "norm2_g")
            dve.wait_ge(g_ps, 1)
            link(dve.tensor_scalar(rows[0:4, 0, :], bw[0][0:4, 0:T], col("b_i")[0:4], None, ALU.add))
            log_sigmoid(0, 4, bw[1][0:4, 0:T], col("b_f")[0:4], lambda i: rows[0:4, 1 + i, :])
            link(dve.memset(rows[0:4, 3, :], 1.0))
            link(dve.tensor_tensor_scan(rows[0:4, 4, :], rows[0:4, 3, :], rows[0:4, 1, :], 0.0, ALU.mult, ALU.add))
            link(dve.tensor_tensor(rows[0:4, 0, :], rows[0:4, 0, :], rows[0:4, 4, :], ALU.subtract))
            link(dve.tensor_tensor_scan(rows[0:4, 1, :], rows[0:4, 3, :], rows[0:4, 0, :], 0.0, ALU.mult, ALU.max))
            dve.tensor_tensor(rows[0:4, 2, :], rows[0:4, 4, :], rows[0:4, 1, :], ALU.add).then_inc(g_scan, 1)
            def merge(sig, first, yv):
                def evict(u, p):
                    s = sig[:, bass.ds(u, 1), :].rearrange("p a t -> p (a t)")
                    d = yv[:, bass.ds(u, 1), :].rearrange("p a t -> p (a t)") if first else s
                    return dve.tensor_tensor(d, p, s, ALU.mult)
                return evict

            attention(0, len(ITEMS1))
            dve.wait_ge(att["y"], len(ITEMS1))
            dve.wait_ge(taken, RUNS["branch_a"].out0)
            dve.wait_ge(used, RUNS["branch_a"].half0)
            split_part(0, yaT)
            run("branch_a", merge(sig1[:, 4:12, :], True, y1))
            dve.wait_ge(g_tr, 1)
            dve.tensor_copy(g_col[:, :, 0:4], bw[0][:, 0:16].rearrange("p (a h) -> p a h", a=2)[:, :, 0:4])\
                .then_inc(g_col_s, 1)
            dve.wait_ge(g_col_s, 1)

            def exponents(h):
                dve.wait_ge(m_s, h + 1)
                if h >= 2:
                    dve.wait_ge(m_o, h - 1)
                for st in range(QT):
                    ins = dve.tensor_scalar(mls_w[:, h % 2, st, :], bw[h % 2][:, 0:T], g_col[:, st, h:h + 1], 0.0,
                                            ALU.subtract, ALU.max)
                ins.then_inc(m_d, 1)

            def weighted(h):
                dve.wait_ge(m_mask, h + 1)
                w = mls_w[:, h % 2, :, :].rearrange("p a t -> p (a t)")
                dve.scalar_tensor_tensor(out=w, in0=bx[h % 2], scalar=P ** -0.5, in1=w, op0=ALU.mult, op1=ALU.mult)\
                    .then_inc(m_w, 1)

            def head_out(h):
                dve.wait_ge(m_o, h + 1)
                o = bx[2 + h % 2]
                d = rstd[:, 0, :]
                link(dve.tensor_scalar(d, o[:, T:2 * T], -1.0, None, ALU.mult))
                link(dve.tensor_tensor(d, d, o[:, T:2 * T], ALU.max))
                link(dve.tensor_tensor(d, d, bw[h % 2][:, T:2 * T], ALU.max))
                link(dve.reciprocal(d, d))
                ins = dve.tensor_tensor(hb[:, h, :], o[:, 0:T], d, ALU.mult)
                ins.then_inc(m_h, 1)
                dve.wait_ge(m_h, h + 1)

            for h in (0, 2):
                for stage in (exponents, weighted, head_out):
                    stage(h)
                    stage(h + 1)
            dve.wait_ge(m_rstd, 1)
            for h in range(4):
                ins = dve.scalar_tensor_tensor(out=hb[:, h, :], in0=hb[:, h, :], scalar=col("mlstm_g", h),
                                               in1=tmp[:, 4 + h, :], op0=ALU.mult, op1=ALU.mult)
            link(ins)
            link(dve.tensor_tensor(ybT, hb, sig1[:, 0:4, :], ALU.mult))
            split_part(4, ybT)
            run("branch_b", merge(sig1[:, 12:20, :], False, y1))
            dve.wait_ge(taken, RUNS["wout1"].out0)
            link(dve.tensor_tensor(y1, y1, sig1[:, 12:20, :], ALU.add))
            split_ready(EV["y1"], (0, y1))

            def add_residual(gate_at):
                def evict(u, p):
                    x = xT[:, bass.ds(u, 1), :].rearrange("p a t -> p (a t)")
                    if gate_at is None:
                        return dve.tensor_tensor(x, p, x, ALU.add)
                    return dve.scalar_tensor_tensor(out=x, in0=p, scalar=mod[:, bass.ds(gate_at + u, 1)], in1=x,
                                                    op0=ALU.mult, op1=ALU.add)
                return evict

            run("wout1", add_residual(16))
            dve.wait_ge(taken, RUNS["pq1"].out0)
            dve.engine_nop().then_inc(x_ready, 1)
            norm_apply("norm2", xT, lambda kt: gain[:, 1, kt:kt + 1], shift_k=1)
            run("pq1")
            experts(1)
            for d in range(KT):
                ins = dve.scalar_tensor_tensor(out=xT[:, d, :], in0=acc[:, d, :], scalar=mod[:, 40 + d:41 + d],
                                               in1=xT[:, d, :], op0=ALU.mult, op1=ALU.add)
                ins.then_inc(x_tile, 1)
            dve.wait_ge(x_tile, KT)
            dve.engine_nop().then_inc(x_ready, 1)
            norm_apply("mem", memT, lambda kt: col("mem_g", kt))
            dve.wait_ge(n_rstd, NORMS.index("final") + 1)
            for kt in range(KT):
                ins = dve.scalar_tensor_tensor(out=xT[:, kt, :], in0=xT[:, kt, :], scalar=col("final_g", kt),
                                               in1=norm_at["final"][1][:, 1, :], op0=ALU.mult, op1=ALU.mult)
            link(ins)
            dve.engine_nop().then_inc(x_ready, 1)
            run("mk")
            run("mv")
            dve.wait_ge(taken, RUNS["fq_fk_sq_mq"].out0)
            dve.wait_ge(swa_d, 1)
            for h in range(8):
                ins = dve.tensor_scalar(biasS[:, h, :, :], dist, -8.0 * 2.0 ** -(h + 1), None, ALU.mult)
            link(ins)
            dve.engine_nop().then_inc(swa_d, 1)
            norm_apply("norm1_2", xT, lambda kt: col("norm1_g_2", kt))
            for name in ("fq_fk_sq_mq", "fv", "sk", "sv", "gates2"):
                run(name)
            dve.wait_ge(g_ps, 2)
            log_sigmoid(1, 8, bw[0][0:8, 0:T], col("b_forget")[0:8], lambda i: rows2[0:8, i, :])
            link(dve.memset(rows2[0:8, 3, :], 1.0))
            dve.tensor_tensor_scan(rows2[0:8, 2, :], rows2[0:8, 3, :], rows2[0:8, 0, :], 0.0, ALU.mult, ALU.add)\
                .then_inc(g_scan, 1)
            dve.wait_ge(g_tr, 2)
            dve.tensor_copy(g_col[:, :, :], bw[0][:, 0:16].rearrange("p (a h) -> p a h", a=2)).then_inc(g_col_s, 1)
            dve.wait_ge(g_col_s, 2)
            for h in range(8):
                dve.wait_ge(fox_bc, h + 1)
                for qt in range(QT):
                    ins = dve.tensor_scalar(biasF[:, h, qt, :], bw[h % 2][:, 0:T], g_col[:, qt, h:h + 1], -8.0,
                                            ALU.subtract, ALU.mult)
                ins.then_inc(dve_fox, 1)
            dve.wait_ge(dve_fox, 8)
            dve.engine_nop().then_inc(fox_d, 1)

            for i in range(len(HEAD_NORMS)):
                src, mat, d, g, n = head_norm(i)
                dve.wait_ge(hn["rstd"], i + 1)
                dve.scalar_tensor_tensor(out=src, in0=src, scalar=g, in1=hn_r[:, i % 4, 0:n], op0=ALU.mult,
                                         op1=ALU.mult).then_inc(hn["out"], 1)
            attention(len(ITEMS1), len(ITEMS))
            dve.wait_ge(att["y"], len(ITEMS))
            dve.wait_ge(used, RUNS["fox_o"].half0)
            split_ready(EV["fox_swa"], (0, oT[:, 0:8, :]))
            run("fox_o", merge(sig2[:, 0:8, :], True, y2))
            dve.wait_ge(used, RUNS["swa_o"].half0)
            split_ready(EV["mem_o"], (0, oT[:, 8:12, :]))
            run("swa_o", merge(sig2[:, 8:16, :], False, y2))
            run("mem_o", merge(sig2[:, 16:24, :], False, y2))
            dve.wait_ge(taken, RUNS["wout2"].out0)
            link(dve.tensor_tensor(y2, y2, sig2[:, 8:16, :], ALU.add))
            link(dve.tensor_tensor(y2, y2, sig2[:, 16:24, :], ALU.add))
            split_ready(EV["y2"], (0, y2))
            run("wout2", add_residual(None))
            dve.wait_ge(taken, RUNS["pq2"].out0)
            dve.engine_nop().then_inc(x_ready, 1)
            norm_apply("norm2_2", xT, lambda kt: col("norm2_g_2", kt))
            run("pq2")
            experts(2)
            for d in range(KT):
                ins = dve.tensor_tensor(xT[:, d, :], acc[:, d, :], xT[:, d, :], ALU.add)
            ins.then_inc(x_ready, 1)


def kernel(**inputs):
    import numpy as np
    import concourse.bacc as bacc
    from concourse.bass_utils import run_bass_kernel_spmd as run

    f = {k: np.asarray(v) for k, v in inputs.items()}

    def units(w):
        return w.reshape(KT, P, -1, P).transpose(2, 1, 0, 3)

    def half_units(w):
        h = w.reshape(4, P, 8, P).transpose(2, 1, 0, 3)
        return h.reshape(4, 2, P, 4, P).transpose(0, 2, 1, 3, 4).reshape(4, P, KT, P)

    def columns(v):
        return v.reshape(-1, P).T

    w_in = f["w_in"][0]
    ka, qa = w_in[:, 512:1024], w_in[:, 0:512]
    va, qkb = w_in[:, 1024:1536], w_in[:, 1536:2560]
    vb, ob = w_in[:, 2560:3072], w_in[:, 3072:3584]
    gates1 = w_in[:, 3584:3592]
    ga_gb = w_in[:, 3592:]
    front1 = np.concatenate([units(ka), units(qa), units(va), units(qkb), units(vb), units(ob),
                             units(ga_gb), half_units(f["w_branch_a"][0]), half_units(f["w_branch_b"][0]),
                             units(f["w_out"][0]), units(f["w_peer_q"][0])])
    w2 = f["w_in_2"][0]
    fq, fk, fv, ff = w2[:, 0:512], w2[:, 512:1024], w2[:, 1024:1536], w2[:, 1536:1544]
    sq, sk, sv = w2[:, 1544:2056], w2[:, 2056:2184], w2[:, 2184:2312]
    mq, gl = w2[:, 2312:2824], w2[:, 2824:]
    sq = sq.reshape(D, 2, 4, 64).transpose(0, 2, 1, 3).reshape(D, 512)
    mkv = f["w_mem_kv_2"][0]
    front2 = np.concatenate([units(mkv[:, 0:512]), units(mkv[:, 512:]), units(fq), units(fk), units(sq), units(mq),
                             units(fv), units(sk), units(sv), units(gl), half_units(f["w_fox_o_2"][0]),
                             half_units(f["w_swa_o_2"][0]), half_units(f["w_mem_o_2"][0]), units(f["w_out_2"][0]),
                             units(f["w_peer_q_2"][0])])
    assert front1.shape[0] == FRONT[1] and front2.shape[0] == FRONT[2]

    def expert_units(u):
        return u.reshape(P, P, KT, P).transpose(1, 3, 2, 0)

    cols = np.zeros((P, N_COLS), np.float32)

    def put(name, a):
        at, n = COLS[name]
        cols[:a.shape[0], at:at + n] = a

    put("b_ada", columns(f["b_ada"][0]))
    put("norm1_g", columns(f["norm1_g"][0]))
    put("norm2_g", columns(f["norm2_g"][0]))
    put("final_g", columns(f["final_g"]))
    put("conv_b", columns(f["conv_b"][0]))
    put("conv_w", f["conv_w"][0].reshape(4, 8, P).transpose(2, 0, 1).reshape(P, 32))
    put("mlstm_g", columns(f["mlstm_norm_g"][0]))
    put("norm1_g_2", columns(f["norm1_g_2"][0]))
    put("b_gate", columns(f["b_gate_2"][0]))
    put("mem_g", columns(f["mem_norm_g_2"][0]))
    put("norm2_g_2", columns(f["norm2_g_2"][0]))
    for name, key in (("fq_g", "fox_q_g_2"), ("fk_g", "fox_k_g_2"), ("sq_g", "swa_q_g_2"), ("sk_g", "swa_k_g_2")):
        put(name, np.tile(f[key][0], 2)[:, None])
    put("mq_g", f["mem_q_g_2"][0][:, None])
    put("mk_g", f["mem_k_g_2"][0][:, None])
    put("sinks", np.tile(f["swa_sinks_2"][0][None, :], (P, 1)))
    put("b_i", f["b_igate"][0][:, None])
    put("b_f", f["b_fgate"][0][:, None])
    put("b_forget", f["b_forget_2"][0][:, None])

    q = np.arange(T)
    rel = np.clip(q[:, None] - q[None, :], -128, 128) + 128
    biasA = f["rel_bias"][0][:, rel].reshape(8, QT, P, T).transpose(2, 0, 1, 3)
    gatew = np.stack([w.reshape(KT, P, 8).transpose(1, 0, 2) for w in (gates1, ff)])
    keys = np.stack([f["peer_sub_keys"][0].reshape(16, P, P).transpose(2, 0, 1),
                     np.stack([f["peer_keys1_2"][0], f["peer_keys2_2"][0]], axis=1).reshape(16, P, P)
                     .transpose(2, 0, 1)])
    arrays = {
        "xT_in": f["x"][0].reshape(T, KT, P).transpose(2, 1, 0),
        "memT_in": f["mem_2"][0].reshape(T, KT, P).transpose(2, 1, 0),
        "cols_in": cols, "front1": front1, "front2": front2,
        "u1": expert_units(f["peer_u"][0]), "v1": f["peer_v"][0].reshape(P, P, D),
        "u2": expert_units(f["peer_u_2"][0]), "v2": f["peer_v_2"][0].reshape(P, P, D),
        "biasA_in": biasA, "gatew_in": gatew, "keys_in": keys,
        "ada_in": f["w_ada"][0].T.reshape(48, P, D), "c_in": f["c"],
    }
    nc = bacc.Bacc("TRN2", target_bir_lowering=False, num_devices=1)
    arrays = {k: np.ascontiguousarray(a) for k, a in arrays.items()}
    args = [nc.dram_tensor(k, a.shape, F32, kind="ExternalInput").ap() for k, a in arrays.items()]
    out = nc.dram_tensor("out_T", (P, KT, T), F32, kind="ExternalOutput").ap()
    two_blocks_kernel(nc, *args, out)
    r = run(nc, [arrays], core_ids=[0])
    return r.results[0]["out_T"].transpose(2, 1, 0).reshape(1, T, D)
```
